# Optimizing a Trainium2 kernel written in Bass

```python
import jax, jax.numpy as jnp
from jax import lax
import numpy as np

D_MODEL = 1024
BATCH = 1
SEQ = 1024
DEPTH = 1
DEC_BATCH = 8
DEC_SEQ = 1
PAST_LEN = 8192
PAGE_SIZE = 128

E_CONV = D_MODEL
E_POOL = D_MODEL
CONV_WIDTH = 31
CONV_BUF = CONV_WIDTH - 1
POOL_WINDOWS = (2, 4, 8, 16)
N_POOL_GROUPS = len(POOL_WINDOWS)
POOL_GROUP = E_POOL // N_POOL_GROUPS
POOL_BUF = max(POOL_WINDOWS) - 1
N_BRANCH = 2
D_IN = 3 * E_CONV + 2 * E_POOL + N_BRANCH * D_MODEL
RMS_EPS = 1e-6
LN_EPS = 1e-5

kernel_name = "conv_pool_gated_hybrid_step"

def rms_norm(x, g):
    xf = x.astype(jnp.float32)
    y = xf * lax.rsqrt(jnp.mean(xf * xf, axis=-1, keepdims=True) + RMS_EPS)
    return (y * g.astype(jnp.float32)).astype(x.dtype)

def layer_norm(x, g, b):
    xf = x.astype(jnp.float32)
    mu = jnp.mean(xf, axis=-1, keepdims=True)
    xc = xf - mu
    var = jnp.mean(xc * xc, axis=-1, keepdims=True)
    y = xc * lax.rsqrt(var + LN_EPS) * g.astype(jnp.float32) + b.astype(jnp.float32)
    return y.astype(x.dtype)

def conv_branch(v, gv, z, buf, w_dw, b_dw, ln_g, ln_b, w_a_out):
    u = v * jax.nn.sigmoid(gv)
    ext = jnp.concatenate([buf.astype(u.dtype), u], axis=1)
    y = lax.conv_general_dilated(ext, w_dw[:, None, :].astype(u.dtype), (1,), "VALID",
                                 dimension_numbers=("NWC", "WIO", "NWC"),
                                 feature_group_count=E_CONV) + b_dw
    y = jax.nn.silu(layer_norm(y, ln_g, ln_b))
    y = y * jax.nn.silu(z)
    return y @ w_a_out, ext[:, -CONV_BUF:]

def pool_branch(u, z, buf, start, w_grp, p_scale, w_b_out):
    B, T, _ = u.shape
    ext = jnp.concatenate([buf.astype(u.dtype), u], axis=1)
    cs = jnp.cumsum(ext.astype(jnp.float32), axis=1)
    cs = jnp.pad(cs, ((0, 0), (1, 0), (0, 0)))
    hi = cs[:, POOL_BUF + 1:POOL_BUF + 1 + T]
    pos = start + jnp.arange(T, dtype=jnp.int32)
    means = []
    for k, w in enumerate(POOL_WINDOWS):
        sl = slice(k * POOL_GROUP, (k + 1) * POOL_GROUP)
        lo = cs[:, POOL_BUF + 1 - w:POOL_BUF + 1 - w + T, sl]
        cnt = jnp.minimum(pos + 1, w).astype(jnp.float32)[None, :, None]
        means.append((hi[..., sl] - lo) / cnt)
    p = (jnp.concatenate(means, axis=-1) - u.astype(jnp.float32)).astype(u.dtype)
    p = p.reshape(B, T, N_POOL_GROUPS, POOL_GROUP)
    y = jnp.einsum("btgc,gcd->btgd", p, w_grp).reshape(B, T, E_POOL) * p_scale
    y = y * jax.nn.silu(z)
    return y @ w_b_out, ext[:, -POOL_BUF:]

def trunk(x, c, conv_bufs, pool_bufs, start, w_ada, b_ada, g_norm, w_in, w_dw, b_dw,
          ln_g, ln_b, w_a_out, w_grp, pool_scale, w_b_out, w_out, g_final):
    new_conv, new_pool = [], []
    c_act = jax.nn.silu(c)
    o1, o2, o3 = E_CONV, 2 * E_CONV, 3 * E_CONV
    o4, o5 = o3 + E_POOL, o3 + 2 * E_POOL
    o6 = o5 + D_MODEL
    for l in range(DEPTH):
        mod = (c_act @ w_ada[l] + b_ada[l])[:, None, :]
        shift, scale, gate = jnp.split(mod, 3, axis=-1)
        h = rms_norm(x, g_norm[l]) * (1 + scale) + shift
        proj = h @ w_in[l]
        y_a, nc = conv_branch(proj[..., :o1], proj[..., o1:o2], proj[..., o2:o3], conv_bufs[l],
                              w_dw[l], b_dw[l], ln_g[l], ln_b[l], w_a_out[l])
        y_b, npl = pool_branch(proj[..., o3:o4], proj[..., o4:o5], pool_bufs[l], start,
                               w_grp[l], pool_scale[l], w_b_out[l])
        m = jax.nn.sigmoid(proj[..., o5:o6]) * y_a + jax.nn.sigmoid(proj[..., o6:]) * y_b
        x = x + gate * (m @ w_out[l])
        new_conv.append(nc)
        new_pool.append(npl)
    return rms_norm(x, g_final), jnp.stack(new_conv), jnp.stack(new_pool)

def setup_inputs(seed: int = 0) -> dict:
    key = jax.random.key(seed)
    ks = jax.random.split(key, 24)
    f32 = jnp.float32
    nrm = lambda k, s, sc: jax.random.normal(k, s, f32) * sc
    return {
        "x_prompt": nrm(ks[0], (BATCH, SEQ, D_MODEL), 1.0),
        "x_sample": nrm(ks[1], (DEC_BATCH, DEC_SEQ, D_MODEL), 1.0),
        "state_conv": nrm(ks[2], (DEPTH, DEC_BATCH, CONV_BUF, E_CONV), 1.0),
        "state_pool": nrm(ks[3], (DEPTH, DEC_BATCH, POOL_BUF, E_POOL), 1.0),
        "c_prompt": nrm(ks[4], (BATCH, D_MODEL), 1.0),
        "c_sample": nrm(ks[5], (DEC_BATCH, D_MODEL), 1.0),
        "w_ada": nrm(ks[6], (DEPTH, D_MODEL, 3 * D_MODEL), 0.5 * D_MODEL ** -0.5),
        "b_ada": nrm(ks[7], (DEPTH, 3 * D_MODEL), 0.01),
        "g_norm": 1.0 + nrm(ks[8], (DEPTH, D_MODEL), 0.02),
        "w_in": nrm(ks[9], (DEPTH, D_MODEL, D_IN), D_MODEL ** -0.5),
        "w_dw": nrm(ks[10], (DEPTH, CONV_WIDTH, E_CONV), CONV_WIDTH ** -0.5),
        "b_dw": nrm(ks[11], (DEPTH, E_CONV), 0.01),
        "ln_g": 1.0 + nrm(ks[12], (DEPTH, E_CONV), 0.02),
        "ln_b": nrm(ks[13], (DEPTH, E_CONV), 0.01),
        "w_a_out": nrm(ks[14], (DEPTH, E_CONV, D_MODEL), E_CONV ** -0.5),
        "w_grp": nrm(ks[15], (DEPTH, N_POOL_GROUPS, POOL_GROUP, POOL_GROUP), POOL_GROUP ** -0.5),
        "pool_scale": 1.0 + nrm(ks[16], (DEPTH, E_POOL), 0.1),
        "w_b_out": nrm(ks[17], (DEPTH, E_POOL, D_MODEL), E_POOL ** -0.5),
        "w_out": nrm(ks[18], (DEPTH, D_MODEL, D_MODEL), D_MODEL ** -0.5),
        "g_final": 1.0 + nrm(ks[19], (D_MODEL,), 0.02),
    }

def reference(x_prompt, x_sample, state_conv, state_pool, c_prompt, c_sample, w_ada, b_ada,
              g_norm, w_in, w_dw, b_dw, ln_g, ln_b, w_a_out, w_grp, pool_scale, w_b_out,
              w_out, g_final):
    params = (w_ada, b_ada, g_norm, w_in, w_dw, b_dw, ln_g, ln_b, w_a_out, w_grp,
              pool_scale, w_b_out, w_out, g_final)
    zc = jnp.zeros((DEPTH, BATCH, CONV_BUF, E_CONV), x_prompt.dtype)
    zp = jnp.zeros((DEPTH, BATCH, POOL_BUF, E_POOL), x_prompt.dtype)
    y_prompt, conv_prompt_new, pool_prompt_new = trunk(x_prompt, c_prompt, zc, zp, 0, *params)
    y_sample, conv_sample_new, pool_sample_new = trunk(x_sample, c_sample, state_conv, state_pool,
                                                       PAST_LEN, *params)
    return (y_prompt, y_sample, conv_prompt_new, conv_sample_new, pool_prompt_new, pool_sample_new)


_drawn_inputs = setup_inputs


def setup_inputs(seed=0):
    import zlib

    import numpy as np

    out = dict(_drawn_inputs(seed))
    spreads = {}
    factors = {'b_ada': 4.135,
     'g_norm': 2.839,
     'b_dw': 8.0,
     'ln_g': 8.0,
     'ln_b': 8.0,
     'pool_scale': 5.896,
     'g_final': 2.836}
    for name, (base, spread) in spreads.items():
        noise = np.random.default_rng([zlib.crc32(name.encode()), seed]).standard_normal(out[name].shape)
        drawn = base * np.exp(spread * noise) if base else spread * noise
        out[name] = __import__('jax').numpy.asarray(drawn.astype(out[name].dtype))
    for name, factor in factors.items():
        out[name] = (out[name] * factor).astype(out[name].dtype)
    return out
```

```python
from contextlib import ExitStack

import concourse.bass as bass
from concourse import mybir

F32 = mybir.dt.float32
F32R = mybir.dt.float32r
ACT = mybir.ActivationFunctionType
ALU = mybir.AluOpType
AX_X = mybir.AxisListType.X

P = 128
D = 1024
SEQ = 1024
NSAMP = 8
TOK = SEQ + NSAMP
CHUNKS = 3
CW = TOK // CHUNKS
KT = D // P
PAIRS = KT // 2
CONV_W = 31
CONV_BUF = CONV_W - 1
POOL_MAX = 16
POOL_BUF = POOL_MAX - 1
DOUBLINGS = 4
NMOD = 1 + NSAMP
ADA_CHUNK = 512
ADA_BLOCKS = ADA_CHUNK // P
RMS_EPS = 1e-6
LN_EPS = 1e-5

PAIR_JOBS = [
    ("glu_gate", 0, "act"), ("glu_value", 0, "dve"), ("glu_gate", 1, "act"), ("glu_value", 1, "dve"),
    ("merge_a", 0, "act"), ("merge_a", 1, "act"), ("merge_b", 0, "act"), ("merge_b", 1, "act"),
    ("pool_in", 0, "act"), ("pool_in", 1, "act"), ("pool_z", 0, "act"), ("pool_z", 1, "act"),
    ("pool_mix", 0, "dve"), ("pool_mix", 1, "dve"), ("conv_z", 0, "act"), ("conv_z", 1, "act"),
]
JOBS_PER_PAIR = len(PAIR_JOBS)
MAIN_PER_PAIR = sum(kind != "pool_mix" for kind, _, _ in PAIR_JOBS)
MIX_WIDTH = 2 * P
PAIR_TOTAL = PAIRS * JOBS_PER_PAIR
JOB_B = PAIR_TOTAL
JOB_A = JOB_B + KT
JOB_OUT = JOB_A + KT
JOBS = JOB_OUT + KT
W_IN_PART = {"glu_value": 0, "glu_gate": 1, "conv_z": 2, "pool_in": 3, "pool_z": 4, "merge_a": 5, "merge_b": 6}

TAPS_AT = {1: (3, 2), 2: (3, 4), 3: (2, 2), 4: (3, 4), 5: (3, 4), 6: (3, 4), 7: (3, 4), 8: (0, 0), 9: (0, 0),
           10: (3, 3), 11: (3, 3), 13: (3, 3)}
assert sum(map(sum, TAPS_AT.values())) == 2 * CONV_W

N_PAR = CONV_W + 2
N_POOLC = DOUBLINGS + 1 + 2 * POOL_MAX


def main_index(i):
    return sum(kind != "pool_mix" for kind, _, _ in PAIR_JOBS[:i])


def evacs(engine, i):
    return sum(e == engine for _, _, e in PAIR_JOBS[:i + 1])


ACT_EVACS = evacs("act", JOBS_PER_PAIR - 1)
DVE_EVACS = evacs("dve", JOBS_PER_PAIR - 1)


def build(nc, t):
    with ExitStack() as ctx:
        base = (nc.sbuf_base + 31) // 32 * 32

        def at(name, shape, dt, offset):
            return nc.alloc_sbuf_tensor_at(name, [P] + shape, dt, offset=offset)

        ROW = TOK * 4
        zone_h = base
        zone_g = zone_h + 2 * KT * ROW
        zone_b = zone_g + 2 * KT * ROW
        zone_rest = zone_b + KT * ROW
        hr = at("hr", [2 * KT, TOK], F32R, zone_h)
        hf = at("hf", [2 * KT, TOK], F32, zone_h)
        gr = at("gr", [2 * KT, TOK], F32R, zone_g)
        gf = at("gf", [2 * KT, TOK], F32, zone_g)
        bf = at("bf", [KT, TOK], F32, zone_b)
        br = at("br", [KT, TOK], F32R, zone_b)
        ada_raw = at("ada_raw", [4, KT, ADA_CHUNK], F32, zone_g)
        cursor = [zone_g]

        def g_place(name, shape, dt):
            size = 4
            for n in shape:
                size *= n
            o = cursor[0]
            cursor[0] += (size + 31) // 32 * 32
            return at(name, shape, dt, o)

        stage_lo = g_place("stage_lo", [2, TOK], F32)
        conv_y = g_place("conv_y", [2, TOK], F32)
        conv_u = g_place("conv_u", [2, CONV_BUF + TOK], F32)
        sig = g_place("sig", [TOK], F32)
        pool_u = g_place("pool_u", [2, POOL_MAX + TOK], F32)
        pool_s = g_place("pool_s", [2, POOL_MAX + SEQ], F32)
        pool_p = g_place("pool_p", [4, TOK], F32R)
        assert cursor[0] <= zone_b
        cursor[0] = zone_rest
        w_raw = g_place("w_raw", [2, KT * P], F32)
        w_hi = g_place("w_hi", [2, KT * P], F32R)
        w_lo = g_place("w_lo", [2, KT * P], F32R)
        row_mean = g_place("row_mean", [TOK], F32)
        stage_hi = g_place("stage_hi", [2, TOK], F32)
        ext_conv = g_place("ext_conv", [2, CONV_W, NSAMP], F32)
        ext_pool = g_place("ext_pool", [2, POOL_MAX, NSAMP], F32)
        prod = g_place("prod", [CONV_W, NSAMP], F32)
        par_all = g_place("par_all", [PAIRS, 2, N_PAR], F32)
        poolc_all = g_place("poolc_all", [PAIRS, N_POOLC], F32)
        par = g_place("par", [2, N_PAR], F32)
        poolc = g_place("poolc", [N_POOLC], F32)
        vecs = g_place("vecs", [4, KT], F32)
        ada_b = g_place("ada_b", [6, ADA_BLOCKS], F32)
        c_in = g_place("c_in", [KT, NMOD], F32)
        c_act = g_place("c_act", [KT, NMOD], F32)
        ident = g_place("ident", [NMOD], F32)
        mod = g_place("mod", [6, ADA_BLOCKS, NMOD], F32)
        ones = g_place("ones", [P], F32)
        eps = g_place("eps", [2], F32)
        assert cursor[0] <= nc.sbuf_usable_end, cursor[0]
        ada_rows = at("ada_rows", [2, ADA_CHUNK], F32, zone_h + KT * ROW)

        stage = [stage_lo[:, 0, :], stage_lo[:, 1, :], stage_hi[:, 0, :], stage_hi[:, 1, :]]
        sq_sum = stage_hi[:, 0, :]
        row_rstd = stage_hi[:, 1, :]
        full_a = stage_hi[:, 1, :]
        G_NORM, LN_G, LN_B, G_FINAL = range(4)

        ps = ctx.enter_context(nc.psum_tensor("ps", [P, 2, CHUNKS, 512], F32))
        aux = ctx.enter_context(nc.psum_tensor("aux", [P, 2, 512], F32))

        def ps_job(s):
            return ps[:, s % 2, :, 0:CW]

        def by_chunk(ap):
            return ap.rearrange("p (c t) -> p c t", c=CHUNKS)

        def cols(c):
            return slice(c * CW, (c + 1) * CW)

        def sem(name):
            return ctx.enter_context(nc.semaphore(name))

        small_loaded = sem("small_loaded")
        par_loaded = sem("par_loaded")
        x_loaded = [sem(f"x_loaded{i}") for i in range(2)]
        ada_loaded = [sem(f"ada_loaded{i}") for i in range(6)]
        raw_full = [sem("raw_full0"), sem("raw_full1")]
        ext_loaded = sem("ext_loaded")
        sigb_loaded = sem("sigb_loaded")
        y_loaded = [sem("y_loaded0"), sem("y_loaded1")]
        siluz_loaded = sem("siluz_loaded")
        siga_loaded = sem("siga_loaded")
        xres_loaded = sem("xres_loaded")
        stage_free = [sem(f"stage_free{i}") for i in range(4)]
        y_free = [sem("y_free0"), sem("y_free1")]
        conv_state_stored = sem("conv_state_stored")
        pool_state_stored = sem("pool_state_stored")
        out_stored = sem("out_stored")
        c_ready = sem("c_ready")
        ones_ready = sem("ones_ready")
        pads_ready = sem("pads_ready")
        ada_done = sem("ada_done")
        ada_rows_ready = sem("ada_rows_ready")
        ada_turned = sem("ada_turned")
        ada_mod_done = sem("ada_mod_done")
        x_squared = sem("x_squared")
        x_summed = sem("x_summed")
        x_var_done = sem("x_var_done")
        x_std_ready = sem("x_std_ready")
        h_full = sem("h_full")
        h_hi_done = sem("h_hi_done")
        h_lo_done = sem("h_lo_done")
        w_hi_done = sem("w_hi_done")
        w_lo_done = sem("w_lo_done")
        pe_done = sem("pe_done")
        act_evac = sem("act_evac")
        dve_evac = sem("dve_evac")
        u_ready = sem("u_ready")
        conv_done = sem("conv_done")
        p_ready = sem("p_ready")
        p_hi_done = sem("p_hi_done")
        p_lo_done = sem("p_lo_done")
        y_summed = sem("y_summed")
        b_hi_done = sem("b_hi_done")
        b_lo_done = sem("b_lo_done")
        mean_done = sem("mean_done")
        mean_ready = sem("mean_ready")
        y_centred = sem("y_centred")
        y_squared = sem("y_squared")
        y_sq_summed = sem("y_sq_summed")
        y_var_done = sem("y_var_done")
        y_std_ready = sem("y_std_ready")
        y_normed = sem("y_normed")
        y_silu = sem("y_silu")
        a_full = sem("a_full")
        a_hi_done = sem("a_hi_done")
        a_lo_done = sem("a_lo_done")
        m_full = sem("m_full")
        m_hi_done = sem("m_hi_done")
        m_lo_done = sem("m_lo_done")
        x_new_ready = sem("x_new_ready")
        x_new_squared = sem("x_new_squared")
        x_new_summed = sem("x_new_summed")
        f_var_done = sem("f_var_done")
        f_std_ready = sem("f_std_ready")
        y_out_ready = sem("y_out_ready")
        dve_chain = sem("dve_chain")

        LINKS = 1 + 2 * (1 + (2 + CONV_W) + (DOUBLINGS + 2 + 1))

        block = ctx.enter_context(nc.Block())

        @block.sync
        def _(sp):
            sp.dma_start(c_in[:], t["c_t"]).then_inc(small_loaded, 16)
            sp.dma_start(ident[0:NMOD, :], t["ident"]).then_inc(small_loaded, 16)
            sp.dma_start(ada_b[:], t["ada_b"]).then_inc(small_loaded, 16)
            sp.dma_start(vecs[:], t["vecs"]).then_inc(small_loaded, 16)
            sp.dma_start(ada_raw[:, 0, :, :], t["w_ada"][0]).then_inc(ada_loaded[0], 16)
            for half in range(2):
                sp.dma_start(bf[:, 4 * half:4 * half + 4, :], t["x_t"][:, 4 * half:4 * half + 4, :]).then_inc(x_loaded[half], 16)
            for q in range(1, 4):
                sp.dma_start(ada_raw[:, q, :, :], t["w_ada"][q]).then_inc(ada_loaded[q], 16)
            for s in range(2):
                sp.dma_start(w_raw[:, s, :], t["w_main"][s]).then_inc(raw_full[s], 16)
            sp.dma_start(par_all[:], t["par"]).then_inc(par_loaded, 16)
            sp.dma_start(poolc_all[:], t["poolc"]).then_inc(par_loaded, 16)
            for q in range(4, 6):
                sp.wait_ge(ada_done, q - 3)
                sp.dma_start(ada_raw[:, q - 4, :, :], t["w_ada"][q]).then_inc(ada_loaded[q], 16)

            with sp.Fori(0, PAIRS) as g:
                sp.wait_ge(conv_state_stored, g * 32 + 32)
                sp.wait_ge(pool_state_stored, g * 32 + 32)
                for i in range(JOBS_PER_PAIR):
                    sp.wait_ge(w_lo_done, g * JOBS_PER_PAIR + (i + 1))
                    n = (i + 2) % JOBS_PER_PAIR
                    if PAIR_JOBS[n][0] == "pool_mix":
                        sp.dma_start(w_raw[:, i % 2, 0:MIX_WIDTH],
                                     t["w_mix"][bass.ds(g * 2 + (n - 12), 1)].rearrange("a p n -> (a p) n")
                                     ).then_inc(raw_full[i % 2], 16)
                    else:
                        k = main_index(n) + (MAIN_PER_PAIR if i + 2 >= JOBS_PER_PAIR else 0)
                        sp.dma_start(w_raw[:, i % 2, :],
                                     t["w_main"][bass.ds(g * MAIN_PER_PAIR + k, 1)].rearrange("a p n -> (a p) n")
                                     ).then_inc(raw_full[i % 2], 16)
                    if i == 0:
                        sp.dma_start(ext_conv[:, :, 0:CONV_BUF, :], t["state_conv"][:, bass.ds(g * 2, 2)]).then_inc(ext_loaded, 16)
                        sp.dma_start(ext_pool[:, :, 0:POOL_BUF, :], t["state_pool"][:, bass.ds(g * 2, 2)]).then_inc(ext_loaded, 16)
                    if i == 8:
                        sp.wait_ge(u_ready, g * 4 + 2)
                        sp.dma_start(t["conv_p"][:, bass.ds(g * 2, 2)], conv_u[:, :, SEQ:SEQ + CONV_BUF]).then_inc(conv_state_stored, 16)
                        sp.dma_start(t["conv_s"][:, bass.ds(g * 2, 2)], ext_conv[:, :, 1:CONV_W, :]).then_inc(conv_state_stored, 16)
                    if i == 12:
                        sp.wait_ge(conv_done, g * 2 + 1)
                        sp.dma_start(t["y_conv"][:, bass.ds(g * 2, 1)], conv_y[:, 0:1, :]).then_inc(y_free[0], 16)
                        sp.wait_ge(u_ready, g * 4 + 4)
                        sp.dma_start(t["pool_p"][:, bass.ds(g * 2, 2)], pool_u[:, :, 1 + SEQ:POOL_MAX + SEQ]).then_inc(pool_state_stored, 16)
                        sp.dma_start(t["pool_s"][:, bass.ds(g * 2, 2)], ext_pool[:, :, 1:POOL_MAX, :]).then_inc(pool_state_stored, 16)
                sp.wait_ge(conv_done, g * 2 + 2)
                sp.dma_start(t["y_conv"][:, bass.ds(g * 2 + 1, 1)], conv_y[:, 1:2, :]).then_inc(y_free[1], 16)

            for half in range(2):
                sp.wait_ge(b_lo_done, 4 * half + 4)
                sp.wait_ge(y_free[half], 16 * (PAIRS + 1))
                if half == 0:
                    sp.wait_ge(y_free[1], 16 * (PAIRS + 1))
                sp.dma_start(bf[:, 4 * half:4 * half + 4, :], t["y_conv"][:, 4 * half:4 * half + 4]).then_inc(y_loaded[half], 16)
            sp.wait_ge(pe_done, PAIR_TOTAL)
            for k in range(4):
                sp.wait_ge(stage_free[k], 16 * (PAIRS if k < 2 else 2 * PAIRS + 1))
            sp.dma_start(hf[:, KT:2 * KT, :], t["sig_b"]).then_inc(sigb_loaded, 16)

            def load_main(s):
                sp.wait_ge(w_lo_done, s - 1)
                sp.dma_start(w_raw[:, s % 2, :], t["w_main"][s - PAIR_TOTAL + PAIRS * MAIN_PER_PAIR]).then_inc(raw_full[s % 2], 16)

            for s in range(JOB_B + 2, JOBS):
                load_main(s)
                if s == JOB_B + 3:
                    sp.wait_ge(y_sq_summed, KT - 1)
                    sp.dma_start(hf[:, 0:KT, :], t["silu_z"]).then_inc(siluz_loaded, 16)
                if s == JOB_A + 1:
                    sp.wait_ge(pe_done, JOB_A)
                    sp.dma_start(gf[:, KT:2 * KT, :], t["sig_a"]).then_inc(siga_loaded, 16)
                if s == JOB_OUT + 1:
                    sp.wait_ge(pe_done, JOB_OUT)
                    sp.dma_start(hf[:, 0:KT, :], t["x_t"]).then_inc(xres_loaded, 16)
            for c in range(CHUNKS):
                sp.wait_ge(y_out_ready, KT * (c + 1))
                sp.dma_start(t["y"][:, :, cols(c)], hf[:, KT:2 * KT, cols(c)]).then_inc(out_stored, 16)
            sp.wait_ge(out_stored, 16 * CHUNKS)
            sp.wait_ge(conv_state_stored, 32 * (PAIRS + 1))
            sp.wait_ge(pool_state_stored, 32 * (PAIRS + 1))

        @block.gpsimd
        def _(pool):
            nc.gpsimd.memset(ones[:], 1.0 / D)
            nc.gpsimd.memset(eps[:, 0:1], RMS_EPS)
            nc.gpsimd.memset(row_mean[:], 0.0)
            nc.gpsimd.memset(eps[:, 1:2], LN_EPS).then_inc(ones_ready, 1)
            pool.wait_ge(ada_done, 6)
            nc.gpsimd.memset(conv_u[:, :, 0:CONV_BUF], 0.0)
            nc.gpsimd.memset(pool_u[:, :, 0:POOL_MAX], 0.0)
            nc.gpsimd.memset(pool_s[:, :, 0:POOL_MAX], 0.0).then_inc(pads_ready, 1)

        @block.tensor
        def _(pe):
            def ada(q):
                pe.wait_ge(ada_loaded[q], 16)
                if q == 0:
                    pe.wait_ge(c_ready, 1)
                if q == 4:
                    pe.wait_ge(x_std_ready, CHUNKS)
                for k in range(KT):
                    last = nc.tensor.matmul(ps[0:NMOD, q // 3, q % 3, :], c_act[:, k, :], ada_raw[:, q % 4, k, :],
                                            start=(k == 0), stop=(k == KT - 1))
                last.then_inc(ada_done, 1)

            def turn(q):
                pe.wait_ge(ada_rows_ready, q + 1)
                for j in range(ADA_BLOCKS):
                    last = nc.tensor.transpose(ps[:, q // 3, q % 3, j * NMOD:(j + 1) * NMOD],
                                               ada_rows[0:NMOD, q % 2, j * P:(j + 1) * P], ident[0:NMOD, :])
                last.then_inc(ada_turned, 1)

            def token_sums(out, row, done):
                nc.tensor.matmul(out, ones[:], row, start=True, stop=True).then_inc(done, 1)

            ada(0)
            ada(1)
            turn(0)
            ada(2)
            turn(1)
            pe.wait_ge(x_summed, 1)
            pe.wait_ge(ones_ready, 1)
            token_sums(aux[:, 0, 0:CW], sq_sum[:, cols(0)], x_var_done)
            token_sums(aux[:, 1, 0:CW], sq_sum[:, cols(1)], x_var_done)
            token_sums(ps[:, 1, 1, 0:CW], sq_sum[:, cols(2)], x_var_done)
            ada(3)
            turn(2)
            turn(3)
            ada(4)
            ada(5)
            turn(4)
            turn(5)

            def k_step(s_par, k, w_cols, rhs_hi, rhs_lo, n_k, chunks=range(CHUNKS)):
                wh = w_hi[:, s_par, w_cols]
                wl = w_lo[:, s_par, w_cols]
                for c in chunks:
                    out = ps[:, s_par, c, 0:CW]
                    nc.tensor.matmul(out, wh, rhs_hi[:, cols(c)], start=(k == 0), stop=False)
                    nc.tensor.matmul(out, wh, rhs_lo[:, cols(c)], start=False, stop=False)
                for c in chunks:
                    last = nc.tensor.matmul(ps[:, s_par, c, 0:CW], wl, rhs_hi[:, cols(c)], start=False, stop=(k == n_k - 1))
                return last

            pe.wait_ge(ada_mod_done, 6)
            with pe.Fori(0, PAIRS) as g:
                for i, (kind, tile, _) in enumerate(PAIR_JOBS):
                    pe.wait_ge(w_lo_done, g * JOBS_PER_PAIR + (i + 1))
                    if i < 2:
                        pe.wait_ge(act_evac, g * ACT_EVACS + (i + 1))
                    elif PAIR_JOBS[i - 2][2] == "act":
                        pe.wait_ge(act_evac, g * ACT_EVACS + (2 + evacs("act", i - 2)))
                    else:
                        pe.wait_ge(dve_evac, g * DVE_EVACS + evacs("dve", i - 2))
                    if kind == "pool_mix":
                        if tile == 0:
                            pe.wait_ge(p_lo_done, g * 2 + 2)
                        for k in range(2):
                            last = k_step(i % 2, k, slice(k * P, (k + 1) * P), pool_p[:, k, :], pool_p[:, 2 + k, :], 2)
                    else:
                        for k in range(KT):
                            if i == 0:
                                pe.wait_ge(h_lo_done, k + 1)
                            last = k_step(i % 2, k, slice(k * P, (k + 1) * P), hr[:, k, :], hr[:, KT + k, :], KT)
                    last.then_inc(pe_done, 1)

            def job(s_par, hi, lo, after_k=None, before_k=None):
                for k in range(KT):
                    if before_k:
                        before_k(k)
                    last = k_step(s_par, k, slice(k * P, (k + 1) * P), hi[k], lo[k], KT)
                    if after_k:
                        after_k(k)
                last.then_inc(pe_done, 1)

            b_hi = [gr[:, k, :] for k in range(KT)]
            b_lo = [gr[:, KT + k, :] for k in range(KT)]

            def mean_third(k):
                if k == 1:
                    pe.wait_ge(mean_ready, 1)
                    token_sums(aux[:, 0, 0:CW], row_mean[:, cols(2)], mean_done)

            def var_third(k):
                if k == 1:
                    pe.wait_ge(y_std_ready, 1)
                    token_sums(aux[:, 0, 0:CW], sq_sum[:, cols(2)], y_var_done)

            pe.wait_ge(y_summed, 2 * PAIRS)
            for c in range(2):
                token_sums(aux[:, c, 0:CW], row_mean[:, cols(c)], mean_done)
            for s in range(JOB_B, JOB_B + 4):
                pe.wait_ge(w_lo_done, s + 1)
                pe.wait_ge(act_evac, 2 + PAIRS * ACT_EVACS)
                if s >= JOB_B + 2:
                    pe.wait_ge(dve_evac, PAIRS * DVE_EVACS + s - 1 - JOB_B)
                if s == JOB_B + 3:
                    pe.wait_ge(y_sq_summed, KT - 1)
                    pe.wait_ge(mean_ready, CHUNKS)
                    for c in range(2):
                        token_sums(aux[:, c, 0:CW], sq_sum[:, cols(c)], y_var_done)
                job(s % 2, b_hi, b_lo,
                    after_k=mean_third if s == JOB_B else var_third if s == JOB_B + 3 else None,
                    before_k=(lambda k: pe.wait_ge(b_lo_done, k + 1)) if s == JOB_B else None)

            def job_pairs(first, count, hi, lo):
                with pe.Fori(0, count // 2) as r:
                    for par_ in range(2):
                        pe.wait_ge(w_lo_done, r * 2 + (first + par_ + 1))
                        pe.wait_ge(dve_evac, r * 2 + (PAIRS * DVE_EVACS + first + par_ - 1 - JOB_B))
                        job((first + par_) % 2, hi, lo)

            job_pairs(JOB_B + 4, KT - 4, b_hi, b_lo)
            pe.wait_ge(a_lo_done, KT)
            job_pairs(JOB_A, KT, [br[:, k, :] for k in range(KT)], [hr[:, k, :] for k in range(KT)])
            m_hi, m_lo = b_hi, b_lo
            for s in range(JOB_OUT, JOB_OUT + 1):
                pe.wait_ge(w_lo_done, s + 1)
                pe.wait_ge(dve_evac, PAIRS * DVE_EVACS + s - 1 - JOB_B)
                job(s % 2, m_hi, m_lo, before_k=lambda k: pe.wait_ge(m_lo_done, k + 1))
            job_pairs(JOB_OUT + 1, KT - 2, m_hi, m_lo)
            s = JOBS - 1
            pe.wait_ge(w_lo_done, s + 1)
            pe.wait_ge(dve_evac, PAIRS * DVE_EVACS + s - 1 - JOB_B)

            def final_var(c):
                pe.wait_ge(x_new_summed, KT - 1 + c)
                token_sums(aux[:, c % 2, 0:CW], sq_sum[:, cols(c)], f_var_done)

            for c in range(CHUNKS):
                for k in range(KT):
                    last = k_step(s % 2, k, slice(k * P, (k + 1) * P), m_hi[k], m_lo[k], KT, chunks=[c])
                last.then_inc(pe_done, 1)
                if c >= 1:
                    final_var(c - 1)
            pe.wait_ge(f_std_ready, 1)
            final_var(2)

        def weight_columns(i):
            return MIX_WIDTH if PAIR_JOBS[i % JOBS_PER_PAIR][0] == "pool_mix" else KT * P

        @block.scalar
        def _(act):
            def split_hi(slot, n, loaded):
                act.wait_ge(raw_full[slot], loaded)
                nc.scalar.activation(w_hi[:, slot, 0:n], w_raw[:, slot, 0:n], ACT.Copy).then_inc(w_hi_done, 1)

            act.wait_ge(small_loaded, 64)
            nc.scalar.activation(c_act[:], c_in[:], ACT.Silu).then_inc(c_ready, 1)

            def ada_out(q):
                act.wait_ge(ada_done, q + 1)
                if q >= 2:
                    act.wait_ge(ada_turned, q - 1)
                nc.scalar.activation(ada_rows[0:NMOD, q % 2, :], ps[0:NMOD, q // 3, q % 3, :], ACT.Copy).then_inc(ada_rows_ready, 1)

            def h_hi(e):
                act.wait_ge(h_full, e + 1)
                nc.scalar.activation(hr[:, e, :], bf[:, e, :], ACT.Copy).then_inc(h_hi_done, 1)

            ada_out(0)
            for e in range(KT):
                act.wait_ge(x_loaded[e // 4], 16)
                nc.scalar.activation(hf[:, e, :], bf[:, e, :], ACT.Square).then_inc(x_squared, 1)
            ada_out(1)
            ada_out(2)
            for s in range(2):
                split_hi(s, KT * P, 16)
            for c in range(CHUNKS):
                src = ps[:, 1, 1, 0:CW] if c == 2 else aux[:, c, 0:CW]
                act.wait_ge(x_var_done, c + 1)
                nc.scalar.activation(row_rstd[:, cols(c)], src, ACT.Sqrt, bias=eps[:, 0:1]).then_inc(x_std_ready, 1)
            h_hi(0)
            h_hi(1)
            ada_out(3)
            for e in range(2, 6):
                h_hi(e)
            ada_out(4)
            ada_out(5)
            for e in range(6, KT):
                h_hi(e)
            act.wait_ge(ada_mod_done, 6)
            act.wait_ge(h_hi_done, KT)
            act.sem_inc(act_evac, 2)
            act.sem_inc(stage_free[2], 16)
            act.sem_inc(stage_free[3], 16)
            act.sem_inc(y_free[0], 16)
            act.sem_inc(y_free[1], 16)
            act.sem_inc(conv_state_stored, 32)
            act.sem_inc(pool_state_stored, 32)

            STAGED = {4: (0, "sig_a"), 5: (1, "sig_a"), 6: (2, "sig_b"), 7: (3, "sig_b"), 14: (2, "silu_z"), 15: (3, "silu_z")}

            def pair_step(g, i):
                kind, tile, engine = PAIR_JOBS[i]
                act.wait_ge(pe_done, g * JOBS_PER_PAIR + (i + 1))
                if engine == "act":
                    src = ps_job(i)
                    if kind == "glu_gate":
                        if tile == 1:
                            act.wait_ge(dve_evac, g * DVE_EVACS + 1)
                        dst, func = sig[:], ACT.Sigmoid
                    elif kind in ("merge_a", "merge_b"):
                        slot = STAGED[i][0]
                        if slot >= 2:
                            act.wait_ge(stage_free[slot], g * 32 + 16)
                        dst, func = stage[slot], ACT.Sigmoid
                    elif kind == "pool_in":
                        if tile == 0:
                            act.wait_ge(pool_state_stored, g * 32 + 32)
                        dst, func = pool_u[:, tile, POOL_MAX:POOL_MAX + TOK], ACT.Copy
                    elif kind == "pool_z":
                        act.wait_ge(stage_free[tile], g * 16 + 16)
                        dst, func = stage[tile], ACT.Silu
                    else:
                        act.wait_ge(stage_free[2 + tile], g * 32 + 32)
                        dst, func = stage[2 + tile], ACT.Silu
                    nc.scalar.activation(by_chunk(dst), src, func).then_inc(act_evac, 1)
                split_hi(i % 2, weight_columns(i + 2), g * (JOBS_PER_PAIR // 2 * 16) + 16 * ((i + 2) // 2 + 1))
                if i in STAGED:
                    slot, name = STAGED[i]
                    act.wait_ge(act_evac, g * ACT_EVACS + (2 + evacs("act", i)))
                    act.dma_start(t[name][:, bass.ds(g * 2 + tile, 1)] if not isinstance(g, int) else t[name][:, 2 * g + tile:2 * g + tile + 1],
                                  stage[slot].rearrange("p (a t) -> p a t", a=1)).then_inc(stage_free[slot], 16)
                if i in (8, 9):
                    act.wait_ge(p_ready, g * 2 + (i - 7))
                    nc.scalar.activation(pool_p[:, tile, :], sig[:], ACT.Copy).then_inc(p_hi_done, 1)

            with act.Fori(0, PAIRS - 1) as g:
                for i in range(JOBS_PER_PAIR):
                    pair_step(g, i)
            for i in range(JOBS_PER_PAIR - 1):
                pair_step(PAIRS - 1, i)
            for e in range(KT):
                if e == 0:
                    act.wait_ge(dve_evac, PAIRS * DVE_EVACS)
                    act.wait_ge(y_free[0], 16 * (PAIRS + 1))
                    act.wait_ge(y_free[1], 16 * (PAIRS + 1))
                    act.wait_ge(conv_state_stored, 32 * (PAIRS + 1))
                    act.wait_ge(pool_state_stored, 32 * (PAIRS + 1))
                    act.wait_ge(p_lo_done, 2 * PAIRS)
                    act.wait_ge(y_summed, 2 * PAIRS)
                nc.scalar.activation(gr[:, e, :], bf[:, e, :], ACT.Copy).then_inc(b_hi_done, 1)
            pair_step(PAIRS - 1, JOBS_PER_PAIR - 1)

            def split_for(s):
                if s + 2 < JOBS:
                    act.wait_ge(pe_done, s + 1)
                    split_hi(s % 2, KT * P, 16 * ((s + 2) // 2 + 1))

            for c in range(CHUNKS):
                act.wait_ge(mean_done, c + 1)
                nc.scalar.activation(row_mean[:, cols(c)], aux[:, c % 2, 0:CW], ACT.Copy).then_inc(mean_ready, 1)
            for e in range(KT):
                if e == 4:
                    split_for(JOB_B)
                act.wait_ge(y_centred, e + 1)
                nc.scalar.activation(hf[:, e, :], bf[:, e, :], ACT.Square).then_inc(y_squared, 1)
            split_for(JOB_B + 1)
            split_for(JOB_B + 2)
            for c in range(CHUNKS):
                act.wait_ge(y_var_done, c + 1)
                nc.scalar.activation(row_rstd[:, cols(c)], aux[:, c % 2, 0:CW], ACT.Sqrt, bias=eps[:, 1:2]).then_inc(y_std_ready, 1)

            def silu_y(e):
                act.wait_ge(y_normed, e + 1)
                nc.scalar.activation(bf[:, e, :], bf[:, e, :], ACT.Silu, bias=vecs[:, LN_B, e:e + 1],
                                     scale=vecs[:, LN_G, e:e + 1]).then_inc(y_silu, 1)

            silu_y(0)
            silu_y(1)
            split_for(JOB_B + 3)
            for e in range(KT):
                act.wait_ge(a_full, e + 1)
                nc.scalar.activation(br[:, e, :], full_a, ACT.Copy).then_inc(a_hi_done, 1)
                if e in (1, 3, 5):
                    split_for(JOB_B + 4 + e // 2)
                if e + 2 < KT:
                    silu_y(e + 2)
            split_for(JOB_B + 7)
            for m in range(KT):
                split_for(JOB_A + m)
                act.wait_ge(m_full, m + 1)
                nc.scalar.activation(gr[:, m, :], hf[:, KT + m, :], ACT.Copy).then_inc(m_hi_done, 1)
            for m in range(KT - 1):
                split_for(JOB_OUT + m)
                act.wait_ge(x_new_ready, m + 1)
                nc.scalar.activation(bf[:, m, :], hf[:, KT + m, :], ACT.Square).then_inc(x_new_squared, 1)
            for c in range(CHUNKS):
                act.wait_ge(x_new_ready, KT + c)
                nc.scalar.activation(bf[:, KT - 1, cols(c)], hf[:, 2 * KT - 1, cols(c)], ACT.Square).then_inc(x_new_squared, 1)
            for c in range(CHUNKS):
                act.wait_ge(f_var_done, c + 1)
                nc.scalar.activation(row_rstd[:, cols(c)], aux[:, c % 2, 0:CW], ACT.Sqrt, bias=eps[:, 0:1]).then_inc(f_std_ready, 1)

        @block.vector
        def _(dve):
            v = nc.vector
            links = [0]
            at_pair = [None]

            def link(ins):
                links[0] += 1
                ins.then_inc(dve_chain, 1)
                g = at_pair[0]
                dve.wait_ge(dve_chain, links[0] if g is None else g * LINKS + links[0])

            def split_lo(slot, n, count):
                dve.wait_ge(w_hi_done, count)
                v.tensor_tensor(w_lo[:, slot, 0:n], w_raw[:, slot, 0:n], w_hi[:, slot, 0:n].bitcast(F32), ALU.subtract).then_inc(w_lo_done, 1)

            def wide(ap, n):
                return ap.unsqueeze(2).broadcast_to([P, ap.shape[1], n])

            for e in range(1, KT):
                dve.wait_ge(x_squared, e + 1)
                link(v.tensor_tensor(sq_sum, hf[:, 0, :] if e == 1 else sq_sum, hf[:, e, :], ALU.add))
            dve.sem_inc(x_summed, 1)

            def modulation(q):
                dve.wait_ge(ada_turned, q + 1)
                link(v.tensor_tensor(mod[:, q, :, :], ps[:, q // 3, q % 3, 0:ADA_BLOCKS * NMOD].rearrange("p (j n) -> p j n", j=ADA_BLOCKS),
                                     wide(ada_b[:, q, :], NMOD), ALU.add))
                if q < 4:
                    link(v.scalar_tensor_tensor(out=mod[:, q, 2:4, :], in0=mod[:, q, 2:4, :], scalar=1.0,
                                                in1=wide(vecs[:, G_NORM, 2 * q:2 * q + 2], NMOD), op0=ALU.add, op1=ALU.mult))
                dve.sem_inc(ada_mod_done, 1)

            dve.wait_ge(small_loaded, 64)
            modulation(0)
            modulation(1)
            for c in range(CHUNKS):
                dve.wait_ge(x_std_ready, c + 1)
                link(v.reciprocal(row_rstd[:, cols(c)], row_rstd[:, cols(c)]))

            def h_tile(e):
                q, j = e // 2, e % 2
                xs = bf[:, e, SEQ:TOK]
                xp = bf[:, e, 0:SEQ]
                v.scalar_tensor_tensor(out=xp, in0=xp, scalar=mod[:, q, 2 + j, 0:1], in1=row_rstd[:, 0:SEQ], op0=ALU.mult, op1=ALU.mult)
                link(v.tensor_tensor(xs, xs, mod[:, q, 2 + j, 1:NMOD], ALU.mult))
                link(v.tensor_tensor(xs, xs, row_rstd[:, SEQ:TOK], ALU.mult))
                v.tensor_scalar(xp, xp, mod[:, q, j, 0:1], None, ALU.add)
                v.tensor_tensor(xs, xs, mod[:, q, j, 1:NMOD], ALU.add).then_inc(h_full, 1)

            def h_lo(e):
                dve.wait_ge(h_hi_done, e + 1)
                v.tensor_tensor(hr[:, KT + e, :], bf[:, e, :], hr[:, e, :].bitcast(F32), ALU.subtract).then_inc(h_lo_done, 1)

            for e in range(KT):
                if e == 4:
                    modulation(2)
                    split_lo(0, KT * P, 1)
                    split_lo(1, KT * P, 2)
                if e == 6:
                    modulation(3)
                h_tile(e)
                if e == 6:
                    dve.wait_ge(ada_turned, 6)
                    for k in range(0, 6):
                        h_lo(k)
            h_lo(6)
            h_lo(7)
            modulation(4)
            modulation(5)
            dve.wait_ge(pads_ready, 1)
            dve.wait_ge(par_loaded, 32)

            base_links = links[0]
            LEVELS = [pool_u, pool_s]

            def tap(x, k):
                y = conv_y[:, x, 0:SEQ]
                if k == 0:
                    return v.tensor_scalar(y, conv_u[:, x, 0:SEQ], par[:, x, 0:1], par[:, x, CONV_W:CONV_W + 1], ALU.mult, ALU.add)
                return v.scalar_tensor_tensor(out=y, in0=conv_u[:, x, k:k + SEQ], scalar=par[:, x, k:k + 1], in1=y, op0=ALU.mult, op1=ALU.add)

            def conv_samples(g, x):
                if x == 0:
                    dve.wait_ge(ext_loaded, g * 32 + 32)
                ys = conv_y[:, x, SEQ:TOK]
                link(v.tensor_tensor(prod[:], ext_conv[:, x, :, :], wide(par[:, x, 0:CONV_W], NSAMP), ALU.mult))
                link(v.tensor_reduce(ys, prod[:].rearrange("p k s -> p s k"), AX_X, ALU.add))
                v.tensor_scalar(ys, ys, par[:, x, CONV_W:CONV_W + 1], None, ALU.add)

            def taps(g, n):
                for _ in range(n):
                    x, k = divmod(tap_at[0], CONV_W)
                    if k == 0:
                        dve.wait_ge(y_free[x], g * 16 + 16)
                        conv_samples(g, x)
                    link(tap(x, k))
                    if k == CONV_W - 1:
                        v.tensor_tensor(row_mean[:], row_mean[:], conv_y[:, x, :], ALU.add).then_inc(y_summed, 1)
                        dve.sem_inc(conv_done, 1)
                    tap_at[0] += 1

            def pool_tile(g, x):
                u = pool_u[:, x, :]
                levels = [u, pool_s[:, 0, :], pool_s[:, 1, :], pool_s[:, 0, :], pool_s[:, 1, :]]
                for n in range(DOUBLINGS):
                    src, dst = levels[n], levels[n + 1]
                    back = 1 << n
                    link(v.scalar_tensor_tensor(out=dst[:, POOL_MAX:POOL_MAX + SEQ], in0=src[:, POOL_MAX - back:POOL_MAX + SEQ - back],
                                                scalar=poolc[:, n:n + 1], in1=src[:, POOL_MAX:POOL_MAX + SEQ], op0=ALU.mult, op1=ALU.add))
                full = sig[:]
                sums = levels[DOUBLINGS]
                v.scalar_tensor_tensor(out=full[:, POOL_MAX:SEQ], in0=sums[:, 2 * POOL_MAX:POOL_MAX + SEQ], scalar=poolc[:, DOUBLINGS:DOUBLINGS + 1],
                                       in1=u[:, 2 * POOL_MAX:POOL_MAX + SEQ], op0=ALU.mult, op1=ALU.subtract)
                inv = poolc[:, DOUBLINGS + 1:DOUBLINGS + 1 + POOL_MAX]
                v.tensor_tensor(full[:, 0:POOL_MAX], sums[:, POOL_MAX:2 * POOL_MAX], inv, ALU.mult)
                win = poolc[:, DOUBLINGS + 1 + POOL_MAX:N_POOLC]
                link(v.tensor_tensor(prod[:, 0:POOL_MAX, :], ext_pool[:, x, :, :], wide(win, NSAMP), ALU.mult))
                link(v.tensor_reduce(full[:, SEQ:TOK], prod[:, 0:POOL_MAX, :].rearrange("p k s -> p s k"), AX_X, ALU.add))
                v.tensor_tensor(full[:, 0:POOL_MAX], full[:, 0:POOL_MAX], u[:, POOL_MAX:2 * POOL_MAX], ALU.subtract)
                v.tensor_tensor(full[:, SEQ:TOK], full[:, SEQ:TOK], u[:, POOL_MAX + SEQ:POOL_MAX + TOK], ALU.subtract).then_inc(p_ready, 1)

            def pool_lo(g, x):
                dve.wait_ge(p_hi_done, g * 2 + (x + 1))
                link(v.tensor_tensor(pool_p[:, 2 + x, :], sig[:], pool_p[:, x, :].bitcast(F32), ALU.subtract))
                dve.sem_inc(p_lo_done, 1)

            tap_at = [0]

            def pair_step(g, i):
                kind, tile, engine = PAIR_JOBS[i]
                dve.wait_ge(pe_done, g * JOBS_PER_PAIR + (i + 1))
                if i == 0:
                    tap_at[0] = 0
                    if isinstance(g, int):
                        v.tensor_copy(par[:], par_all[:, g, :, :])
                        link(v.tensor_copy(poolc[:], poolc_all[:, g, :]))
                    else:
                        v.tensor_copy(par[:], par_all[:, bass.ds(g, 1), :, :].rearrange("p a x n -> p (a x) n"))
                        link(v.tensor_copy(poolc[:], poolc_all[:, bass.ds(g, 1), :].rearrange("p a n -> p (a n)")))
                if kind == "glu_value":
                    dve.wait_ge(act_evac, g * ACT_EVACS + (2 + evacs("act", i - 1)))
                    if tile == 0:
                        dve.wait_ge(conv_state_stored, g * 32 + 32)
                        dve.wait_ge(ext_loaded, g * 32 + 32)
                    link(v.tensor_tensor(by_chunk(conv_u[:, tile, CONV_BUF:CONV_BUF + TOK]), ps_job(i), by_chunk(sig[:]), ALU.mult))
                    dve.sem_inc(dve_evac, 1)
                    v.tensor_copy(ext_conv[:, tile, CONV_BUF, :], conv_u[:, tile, CONV_BUF + SEQ:CONV_BUF + TOK]).then_inc(u_ready, 1)
                    dve.wait_ge(u_ready, g * 4 + (tile + 1))
                if kind == "pool_mix":
                    dve.wait_ge(act_evac, g * ACT_EVACS + (2 + evacs("act", 10 + tile)))
                    e = g * 2 + tile
                    dst = bf[:, e, :] if isinstance(g, int) else bf[:, bass.ds(e, 1), :].rearrange("p a t -> p (a t)")
                    v.scalar_tensor_tensor(out=by_chunk(dst), in0=ps_job(i), scalar=par[:, tile, CONV_W + 1:CONV_W + 2],
                                           in1=by_chunk(stage[tile]), op0=ALU.mult, op1=ALU.mult).then_inc(dve_evac, 1)
                before, after = TAPS_AT.get(i, (0, 0))
                taps(g, before)
                if i in (8, 9):
                    dve.wait_ge(act_evac, g * ACT_EVACS + (2 + evacs("act", i)))
                    if tile == 1:
                        pool_lo(g, 0)
                    v.tensor_copy(ext_pool[:, tile, POOL_BUF, :], pool_u[:, tile, POOL_MAX + SEQ:POOL_MAX + TOK]).then_inc(u_ready, 1)
                    pool_tile(g, tile)
                if i == 10:
                    pool_lo(g, 1)
                split_lo(i % 2, weight_columns(i + 2), g * JOBS_PER_PAIR + (i + 3))
                taps(g, after)

            with dve.Fori(0, PAIRS - 1) as g:
                at_pair[0] = g
                for i in range(JOBS_PER_PAIR):
                    pair_step(g, i)
                assert links[0] - base_links == LINKS, (links[0] - base_links, LINKS)
            at_pair[0] = None
            links[0] = base_links + (PAIRS - 1) * LINKS
            for i in range(JOBS_PER_PAIR - 1):
                pair_step(PAIRS - 1, i)
            for e in range(KT):
                dve.wait_ge(b_hi_done, e + 1)
                v.tensor_tensor(gr[:, KT + e, :], bf[:, e, :], gr[:, e, :].bitcast(F32), ALU.subtract).then_inc(b_lo_done, 1)
            pair_step(PAIRS - 1, JOBS_PER_PAIR - 1)

            def split_for(s):
                if s + 2 < JOBS:
                    split_lo(s % 2, KT * P, s + 3)

            def merge_b(m):
                s = JOB_B + m
                dve.wait_ge(pe_done, s + 1)
                dve.wait_ge(sigb_loaded, 16)
                row = hf[:, KT + m, :]
                v.tensor_tensor(by_chunk(row), ps_job(s), by_chunk(row), ALU.mult).then_inc(dve_evac, 1)

            dve.wait_ge(mean_ready, CHUNKS)
            for e in range(KT):
                dve.wait_ge(y_loaded[e // 4], 16)
                v.tensor_tensor(bf[:, e, :], bf[:, e, :], row_mean[:], ALU.subtract).then_inc(y_centred, 1)
                if e == 5:
                    merge_b(0)
                    split_for(JOB_B)
            for e in range(1, KT):
                dve.wait_ge(y_squared, e + 1)
                v.tensor_tensor(sq_sum, hf[:, 0, :] if e == 1 else sq_sum, hf[:, e, :], ALU.add).then_inc(y_sq_summed, 1)
                dve.wait_ge(y_sq_summed, e)
            merge_b(1)
            split_for(JOB_B + 1)
            merge_b(2)
            split_for(JOB_B + 2)
            for c in range(CHUNKS):
                dve.wait_ge(y_std_ready, c + 1)
                link(v.reciprocal(row_rstd[:, cols(c)], row_rstd[:, cols(c)]))
            for e in range(KT):
                if e == 3:
                    merge_b(3)
                    split_for(JOB_B + 3)
                last = v.tensor_tensor(bf[:, e, :], bf[:, e, :], row_rstd, ALU.mult)
                last.then_inc(y_normed, 1)
            dve.wait_ge(siluz_loaded, 16)
            dve.wait_ge(y_normed, KT)
            for e in range(KT):
                dve.wait_ge(y_silu, e + 1)
                v.tensor_tensor(full_a, bf[:, e, :], hf[:, e, :], ALU.mult).then_inc(a_full, 1)
                if e in (1, 3, 5):
                    merge_b(4 + e // 2)
                    split_for(JOB_B + 4 + e // 2)
                dve.wait_ge(a_hi_done, e + 1)
                link(v.tensor_tensor(hr[:, e, :], full_a, br[:, e, :].bitcast(F32), ALU.subtract))
                dve.sem_inc(a_lo_done, 1)
            merge_b(7)
            split_for(JOB_B + 7)

            for m in range(KT):
                s = JOB_A + m
                dve.wait_ge(pe_done, s + 1)
                dve.wait_ge(siga_loaded, 16)
                t_row, m_row = gf[:, KT + m, :], hf[:, KT + m, :]
                v.tensor_tensor(by_chunk(t_row), ps_job(s), by_chunk(t_row), ALU.mult).then_inc(dve_evac, 1)
                dve.wait_ge(dve_evac, PAIRS * DVE_EVACS + s + 1 - JOB_B)
                v.tensor_tensor(m_row, t_row, m_row, ALU.add).then_inc(m_full, 1)
                split_for(s)
                dve.wait_ge(m_hi_done, m + 1)
                v.tensor_tensor(gr[:, KT + m, :], m_row, gr[:, m, :].bitcast(F32), ALU.subtract).then_inc(m_lo_done, 1)

            def new_x(m, c0, c1):
                gate = mod[:, 4 + m // 4, m % 4, :]
                hi = min(c1 * CW, SEQ)
                for c in range(c0, c1):
                    w = min(CW, SEQ - c * CW)
                    last = v.scalar_tensor_tensor(out=hf[:, KT + m, c * CW:c * CW + w], in0=ps[:, (JOB_OUT + m) % 2, c, 0:w],
                                                  scalar=gate[:, 0:1], in1=hf[:, m, c * CW:c * CW + w], op0=ALU.mult, op1=ALU.add)
                if c1 == CHUNKS:
                    xs = hf[:, KT + m, SEQ:TOK]
                    link(v.tensor_tensor(xs, ps[:, (JOB_OUT + m) % 2, CHUNKS - 1, CW - NSAMP:CW], gate[:, 1:NMOD], ALU.mult))
                    last = v.tensor_tensor(xs, xs, hf[:, m, SEQ:TOK], ALU.add)
                return last

            dve.wait_ge(xres_loaded, 16)
            for m in range(KT - 1):
                dve.wait_ge(pe_done, JOB_OUT + m + 1)
                link(new_x(m, 0, CHUNKS))
                dve.sem_inc(dve_evac, 1)
                dve.sem_inc(x_new_ready, 1)
                split_for(JOB_OUT + m)
                if m >= 1:
                    dve.wait_ge(x_new_squared, m + 1)
                    link(v.tensor_tensor(sq_sum, bf[:, 0, :] if m == 1 else sq_sum, bf[:, m, :], ALU.add))
            dve.sem_inc(x_new_summed, KT - 2)

            def norm_out(c):
                dve.wait_ge(f_std_ready, c + 1)
                link(v.reciprocal(row_rstd[:, cols(c)], row_rstd[:, cols(c)]))
                for m in range(KT):
                    row = hf[:, KT + m, cols(c)]
                    v.scalar_tensor_tensor(out=row, in0=row, scalar=vecs[:, G_FINAL, m:m + 1], in1=row_rstd[:, cols(c)],
                                           op0=ALU.mult, op1=ALU.mult).then_inc(y_out_ready, 1)

            for c in range(CHUNKS):
                dve.wait_ge(pe_done, JOBS + c)
                new_x(KT - 1, c, c + 1).then_inc(x_new_ready, 1)
                dve.wait_ge(x_new_squared, KT + c)
                v.tensor_tensor(sq_sum[:, cols(c)], sq_sum[:, cols(c)], bf[:, KT - 1, cols(c)], ALU.add).then_inc(x_new_summed, 1)
            for c in range(CHUNKS):
                norm_out(c)


def kernel(**inputs):
    import numpy as np
    import concourse.bacc as bacc
    from concourse.bass_utils import run_bass_kernel_spmd

    a = {k: np.asarray(v) for k, v in inputs.items()}
    cat = np.concatenate

    def channel_major(x):
        return x.T.reshape(KT, P, -1).transpose(1, 0, 2)

    def column_blocks(w, width=P):
        k, n = w.shape
        return w.reshape(k // P, P, n // width, width).transpose(2, 1, 0, 3).reshape(n // width, P, -1)

    w_in = {kind: column_blocks(a["w_in"][0][:, part * D:(part + 1) * D]) for kind, part in W_IN_PART.items()}
    main = [w_in[kind][2 * g + tile] for g in range(PAIRS) for kind, tile, _ in PAIR_JOBS if kind != "pool_mix"]
    main = cat([np.stack(main), column_blocks(a["w_b_out"][0]), column_blocks(a["w_a_out"][0]), column_blocks(a["w_out"][0])])
    mix = cat([column_blocks(a["w_grp"][0][g]) for g in range(PAIRS)])

    w_ada, b_ada = a["w_ada"][0], a["b_ada"][0]
    order = [np.arange(part * D + 2 * q * P, part * D + (2 * q + 2) * P) for q in range(PAIRS) for part in (0, 1)]
    order = cat(order + [np.arange(2 * D, 3 * D)])
    ada = column_blocks(w_ada[:, order], ADA_CHUNK).reshape(6, P, KT, ADA_CHUNK)
    ada_b = b_ada[order].reshape(6, ADA_BLOCKS, P).transpose(2, 0, 1)

    def column(x):
        return x.reshape(KT, P).T

    par = cat([a["w_dw"][0], a["b_dw"], a["pool_scale"]])
    par = channel_major(par).reshape(P, PAIRS, 2, N_PAR)
    poolc = np.zeros((P, PAIRS, N_POOLC), np.float32)
    for g in range(PAIRS):
        w = 2 << g
        poolc[:, g, 0:g + 1] = 1.0
        poolc[:, g, DOUBLINGS] = 1.0 / w
        poolc[:, g, DOUBLINGS + 1:DOUBLINGS + 1 + POOL_MAX] = 1.0 / np.minimum(np.arange(POOL_MAX) + 1, w)
        poolc[:, g, N_POOLC - w:] = 1.0 / w

    def state(x):
        return x.transpose(2, 1, 0).reshape(KT, P, x.shape[1], NSAMP).transpose(1, 0, 2, 3)

    sent = {
        "x_t": channel_major(cat([a["x_prompt"][0], a["x_sample"][:, 0]])),
        "c_t": channel_major(cat([a["c_prompt"], a["c_sample"]])),
        "ident": np.eye(NMOD, dtype=np.float32),
        "w_ada": ada, "ada_b": ada_b, "w_main": main, "w_mix": mix,
        "vecs": np.stack([column(a["g_norm"][0]), column(a["ln_g"][0]), column(a["ln_b"][0]), column(a["g_final"])], 1),
        "par": par, "poolc": poolc,
        "state_conv": state(a["state_conv"][0]), "state_pool": state(a["state_pool"][0]),
    }
    sent = {k: np.ascontiguousarray(v) for k, v in sent.items()}
    nc = bacc.Bacc("TRN2", target_bir_lowering=False, num_devices=1)
    t = {k: nc.dram_tensor(k, v.shape, F32, kind="ExternalInput").ap() for k, v in sent.items()}
    outs = {"y": [P, KT, TOK], "conv_p": [P, KT, CONV_BUF], "conv_s": [P, KT, CONV_BUF, NSAMP],
            "pool_p": [P, KT, POOL_BUF], "pool_s": [P, KT, POOL_BUF, NSAMP]}
    for k, shape in outs.items():
        t[k] = nc.dram_tensor(k, shape, F32, kind="ExternalOutput").ap()
    for k in ("y_conv", "sig_a", "sig_b", "silu_z"):
        t[k] = nc.dram_tensor(k, [P, KT, TOK], F32, kind="Internal").ap()
    build(nc, t)
    r = run_bass_kernel_spmd(nc, [sent], core_ids=[0]).results[0]

    def rows(x):
        return x.transpose(2, 1, 0).reshape(x.shape[2], D)

    y = rows(r["y"])
    samples = {k: r[k].transpose(3, 2, 1, 0).reshape(1, NSAMP, -1, D) for k in ("conv_s", "pool_s")}
    return (y[None, :SEQ], y[SEQ:, None], rows(r["conv_p"])[None, None], samples["conv_s"],
            rows(r["pool_p"])[None, None], samples["pool_s"])
```

```python
from contextlib import ExitStack

import concourse.bass as bass
from concourse import mybir

F32 = mybir.dt.float32
F32R = mybir.dt.float32r
ACT = mybir.ActivationFunctionType
ALU = mybir.AluOpType
AX_X = mybir.AxisListType.X

P = 128
D = 1024
SEQ = 1024
NSAMP = 8
TOK = SEQ + NSAMP
CHUNKS = 3
CW = TOK // CHUNKS
KT = D // P
PAIRS = KT // 2
CONV_W = 31
CONV_BUF = CONV_W - 1
POOL_MAX = 16
POOL_BUF = POOL_MAX - 1
DOUBLINGS = 4
NMOD = 1 + NSAMP
ADA_CHUNK = 512
ADA_BLOCKS = ADA_CHUNK // P
QUAD = 32
QUADS = P // QUAD
RMS_EPS = 1e-6
LN_EPS = 1e-5

PAIR_JOBS = [
    ("glu_gate", 0, "act"), ("glu_value", 0, "dve"), ("glu_gate", 1, "act"), ("glu_value", 1, "dve"),
    ("merge_a", 0, "act"), ("merge_a", 1, "act"), ("merge_b", 0, "act"), ("merge_b", 1, "act"),
    ("pool_in", 0, "act"), ("pool_in", 1, "act"), ("pool_z", 0, "act"), ("pool_z", 1, "act"),
    ("pool_mix", 0, "dve"), ("conv_z", 0, "act"), ("pool_mix", 1, "dve"), ("conv_z", 1, "act"),
]
JOBS_PER_PAIR = len(PAIR_JOBS)
MAIN_PER_PAIR = sum(kind != "pool_mix" for kind, _, _ in PAIR_JOBS)
MIX_WIDTH = 2 * P
PAIR_TOTAL = PAIRS * JOBS_PER_PAIR
JOB_B = PAIR_TOTAL
JOB_A = JOB_B + KT
JOB_OUT = JOB_A + KT
JOBS = JOB_OUT + KT
W_IN_PART = {"glu_value": 0, "glu_gate": 1, "conv_z": 2, "pool_in": 3, "pool_z": 4, "merge_a": 5, "merge_b": 6}

TAPS_AT = {1: (1, 4), 2: (2, 5), 3: (0, 5), 4: (2, 5), 5: (2, 5), 6: (2, 5), 7: (2, 5), 8: (0, 1), 9: (0, 1), 10: (0, 4),
           12: (0, 6), 14: (0, 5)}
LAST_TAPS_AT = {1: (1, 5), 2: (2, 5), 3: (0, 5), 4: (2, 5), 5: (2, 5), 6: (2, 5), 7: (2, 6), 8: (0, 1), 9: (0, 1), 10: (0, 3),
                11: (0, 2), 12: (0, 6), 13: (0, 2)}
assert sum(map(sum, TAPS_AT.values())) == sum(map(sum, LAST_TAPS_AT.values())) == 2 * CONV_W

SHORT_NEXT = [i for i in range(JOBS_PER_PAIR - 1) if PAIR_JOBS[i + 1][0] == "pool_mix"]

WARM_SUMS = 10
WARM_ADA = ((0, 4), (0, 8), (0, 0), (0, 0))
WARM_TURN = (3, 3, 0, 0)
WARM_FINAL = 22

OUT_STORES = [(0, 0, KT), (1, 0, KT), (2, 0, 4), (2, 4, 6), (2, 6, KT)]

N_PAR = CONV_W + 2
N_POOLC = DOUBLINGS + 1 + 2 * POOL_MAX


def main_index(i):
    return sum(kind != "pool_mix" for kind, _, _ in PAIR_JOBS[:i])


def evacs(engine, i):
    return sum(e == engine for _, _, e in PAIR_JOBS[:i + 1])


ACT_EVACS = evacs("act", JOBS_PER_PAIR - 1)
DVE_EVACS = evacs("dve", JOBS_PER_PAIR - 1)


def build(nc, t):
    with ExitStack() as ctx:
        base = (nc.sbuf_base + 31) // 32 * 32

        def at(name, shape, dt, offset):
            return nc.alloc_sbuf_tensor_at(name, [P] + shape, dt, offset=offset)

        ROW = TOK * 4
        zone_h = base
        zone_g = zone_h + 2 * KT * ROW
        zone_b = zone_g + 2 * KT * ROW
        zone_rest = zone_b + KT * ROW
        hr = at("hr", [2 * KT, TOK], F32R, zone_h)
        hf = at("hf", [2 * KT, TOK], F32, zone_h)
        gr = at("gr", [2 * KT, TOK], F32R, zone_g)
        gf = at("gf", [2 * KT, TOK], F32, zone_g)
        bf = at("bf", [KT, TOK], F32, zone_b)
        br = at("br", [KT, TOK], F32R, zone_b)
        ada_raw = at("ada_raw", [4, KT, ADA_CHUNK], F32, zone_g)
        cursor = [zone_g]

        def g_place(name, shape, dt):
            size = 4
            for n in shape:
                size *= n
            o = cursor[0]
            cursor[0] += (size + 31) // 32 * 32
            return at(name, shape, dt, o)

        stage_lo = g_place("stage_lo", [2, TOK], F32)
        conv_y = g_place("conv_y", [2, TOK], F32)
        conv_u = g_place("conv_u", [2, CONV_BUF + TOK], F32)
        sig = g_place("sig", [TOK], F32)
        pool_u = g_place("pool_u", [2, POOL_MAX + TOK], F32)
        pool_s = g_place("pool_s", [2, POOL_MAX + SEQ], F32)
        pool_p = g_place("pool_p", [4, TOK], F32R)
        assert cursor[0] <= zone_b
        cursor[0] = zone_rest
        w_raw = g_place("w_raw", [2, KT * P], F32)
        w_hi = g_place("w_hi", [2, KT * P], F32R)
        w_lo = g_place("w_lo", [2, KT * P], F32R)
        row_mean = g_place("row_mean", [TOK], F32)
        stage_hi = g_place("stage_hi", [2, TOK], F32)
        ext_at = cursor[0]
        ext_conv = g_place("ext_conv", [2, CONV_W, NSAMP], F32)
        ext_pool = g_place("ext_pool", [2, POOL_MAX, NSAMP], F32)
        prod = g_place("prod", [CONV_W, NSAMP], F32)
        par_all = g_place("par_all", [PAIRS, 2, N_PAR], F32)
        poolc_all = g_place("poolc_all", [PAIRS, N_POOLC], F32)
        par = g_place("par", [2, N_PAR], F32)
        poolc = g_place("poolc", [N_POOLC], F32)
        vecs = g_place("vecs", [4, KT], F32)
        ada_b = g_place("ada_b", [6, ADA_BLOCKS], F32)
        c_in = g_place("c_in", [KT, NMOD], F32)
        c_act = g_place("c_act", [KT, QUAD], F32)
        pick = g_place("pick", [NMOD], F32)
        mod = g_place("mod", [6, ADA_BLOCKS, NMOD], F32)
        ones = g_place("ones", [P], F32)
        eps = g_place("eps", [2], F32)
        assert cursor[0] <= nc.sbuf_usable_end, cursor[0]
        ada_rows = at("ada_rows", [2, ADA_CHUNK], F32, zone_h + (2 * KT - 2) * ROW)
        gate_raw = at("gate_raw", [KT, ADA_CHUNK], F32, zone_g + 4 * ROW)
        gate_rows = at("gate_rows", [ADA_CHUNK], F32, ext_at)

        stage = [stage_lo[:, 0, :], stage_lo[:, 1, :], stage_hi[:, 0, :], stage_hi[:, 1, :]]
        sq_sum = stage_hi[:, 0, :]
        row_rstd = stage_hi[:, 1, :]
        full_a = stage_hi[:, 1, :]
        G_NORM, LN_G, LN_B, G_FINAL = range(4)

        ps = ctx.enter_context(nc.psum_tensor("ps", [P, 2, CHUNKS, 512], F32))
        aux = ctx.enter_context(nc.psum_tensor("aux", [P, 2, 512], F32))

        def ps_job(s):
            return ps[:, s % 2, :, 0:CW]

        ada_bank = [ps[:, 1, 0, :], ps[:, 1, 2, :], aux[:, 1, :], aux[:, 0, :]]

        def by_chunk(ap):
            return ap.rearrange("p (c t) -> p c t", c=CHUNKS)

        def cols(c):
            return slice(c * CW, (c + 1) * CW)

        def sem(name):
            return ctx.enter_context(nc.semaphore(name))

        small_loaded = sem("small_loaded")
        par_loaded = sem("par_loaded")
        x_loaded = [sem(f"x_loaded{i}") for i in range(4)]
        ada_loaded = [[sem(f"ada_loaded{i}_{half}") for half in range(2)] for i in range(4)]
        gate_loaded = sem("gate_loaded")
        raw_full = [sem("raw_full0"), sem("raw_full1")]
        ext_loaded = sem("ext_loaded")
        sigb_loaded = [sem(f"sigb_loaded{i}") for i in range(4)]
        y_loaded = [sem(f"y_loaded{i}") for i in range(4)]
        siluz_loaded = sem("siluz_loaded")
        siga_loaded = [sem("siga_loaded0"), sem("siga_loaded1")]
        xres_loaded = [sem("xres_loaded0"), sem("xres_loaded1")]
        stage_free = [sem(f"stage_free{i}") for i in range(4)]
        y_free = [sem("y_free0"), sem("y_free1")]
        conv_state_stored = sem("conv_state_stored")
        pool_state_stored = sem("pool_state_stored")
        out_stored = sem("out_stored")
        c_padded = sem("c_padded")
        c_ready = sem("c_ready")
        ones_ready = sem("ones_ready")
        pads_ready = sem("pads_ready")
        ada_done = sem("ada_done")
        ada_rows_ready = sem("ada_rows_ready")
        ada_turned = sem("ada_turned")
        ada_mod_done = sem("ada_mod_done")
        x_squared = sem("x_squared")
        x_summed = sem("x_summed")
        x_var_done = sem("x_var_done")
        x_std_ready = sem("x_std_ready")
        h_scaled = sem("h_scaled")
        h_shifted = sem("h_shifted")
        h_hi_done = sem("h_hi_done")
        h_lo_done = sem("h_lo_done")
        gate_done = sem("gate_done")
        gate_rows_ready = sem("gate_rows_ready")
        gate_turned = sem("gate_turned")
        gate_ready = sem("gate_ready")
        w_hi_done = sem("w_hi_done")
        w_lo_done = sem("w_lo_done")
        pe_done = sem("pe_done")
        act_evac = sem("act_evac")
        dve_evac = sem("dve_evac")
        u_ready = sem("u_ready")
        conv_done = sem("conv_done")
        p_ready = sem("p_ready")
        p_hi_done = sem("p_hi_done")
        p_lo_done = sem("p_lo_done")
        y_summed = sem("y_summed")
        b_hi_done = sem("b_hi_done")
        b_lo_done = sem("b_lo_done")
        mean_done = sem("mean_done")
        mean_ready = sem("mean_ready")
        y_centred = sem("y_centred")
        y_squared = sem("y_squared")
        y_sq_summed = sem("y_sq_summed")
        y_var_done = sem("y_var_done")
        y_std_ready = sem("y_std_ready")
        y_normed = sem("y_normed")
        y_silu = sem("y_silu")
        a_full = sem("a_full")
        a_hi_done = sem("a_hi_done")
        a_lo_done = sem("a_lo_done")
        m_full = sem("m_full")
        m_hi_done = sem("m_hi_done")
        m_lo_done = sem("m_lo_done")
        x_new_ready = sem("x_new_ready")
        x_new_squared = sem("x_new_squared")
        x_new_summed = sem("x_new_summed")
        f_var_done = sem("f_var_done")
        f_std_ready = sem("f_std_ready")
        y_out_ready = sem("y_out_ready")
        dve_chain = sem("dve_chain")

        LINKS = 1 + 2 * (1 + (2 + CONV_W) + (DOUBLINGS + 2 + 1))

        block = ctx.enter_context(nc.Block())

        @block.sync
        def _(sp):
            sp.dma_start(c_in[:], t["c_t"]).then_inc(small_loaded, 16)
            sp.dma_start(pick[:], t["pick"]).then_inc(small_loaded, 16)
            sp.dma_start(ada_b[:], t["ada_b"]).then_inc(small_loaded, 16)
            sp.dma_start(vecs[:], t["vecs"]).then_inc(small_loaded, 16)
            for n in range(4):
                sp.dma_start(bf[:, 2 * n:2 * n + 2, :], t["x_t"][:, 2 * n:2 * n + 2, :]).then_inc(x_loaded[n], 16)
            for s in range(2):
                sp.dma_start(w_raw[:, s, :], t["w_main"][s]).then_inc(raw_full[s], 16)
            for q in range(4):
                for half in range(2):
                    k = slice(half * KT // 2, (half + 1) * KT // 2)
                    sp.dma_start(ada_raw[:, q, k, :], t["w_ada"][q][:, k, :]).then_inc(ada_loaded[q][half], 16)
            sp.dma_start(par_all[:], t["par"]).then_inc(par_loaded, 16)
            sp.dma_start(poolc_all[:], t["poolc"]).then_inc(par_loaded, 16)

            with sp.Fori(0, PAIRS) as g:
                sp.wait_ge(conv_state_stored, g * 32 + 32)
                sp.wait_ge(pool_state_stored, g * 32 + 32)
                for i in range(JOBS_PER_PAIR):
                    sp.wait_ge(w_lo_done, g * JOBS_PER_PAIR + (i + 1))
                    n = (i + 2) % JOBS_PER_PAIR
                    if PAIR_JOBS[n][0] == "pool_mix":
                        sp.dma_start(w_raw[:, i % 2, 0:MIX_WIDTH],
                                     t["w_mix"][bass.ds(g * 2 + PAIR_JOBS[n][1], 1)].rearrange("a p n -> (a p) n")
                                     ).then_inc(raw_full[i % 2], 16)
                    else:
                        k = main_index(n) + (MAIN_PER_PAIR if i + 2 >= JOBS_PER_PAIR else 0)
                        sp.dma_start(w_raw[:, i % 2, :],
                                     t["w_main"][bass.ds(g * MAIN_PER_PAIR + k, 1)].rearrange("a p n -> (a p) n")
                                     ).then_inc(raw_full[i % 2], 16)
                    if i == 0:
                        sp.dma_start(ext_conv[:, :, 0:CONV_BUF, :], t["state_conv"][:, bass.ds(g * 2, 2)]).then_inc(ext_loaded, 16)
                        sp.dma_start(ext_pool[:, :, 0:POOL_BUF, :], t["state_pool"][:, bass.ds(g * 2, 2)]).then_inc(ext_loaded, 16)
                    if i == 8:
                        sp.wait_ge(u_ready, g * 4 + 2)
                        sp.dma_start(t["conv_p"][:, bass.ds(g * 2, 2)], conv_u[:, :, SEQ:SEQ + CONV_BUF]).then_inc(conv_state_stored, 16)
                        sp.dma_start(t["conv_s"][:, bass.ds(g * 2, 2)], ext_conv[:, :, 1:CONV_W, :]).then_inc(conv_state_stored, 16)
                    if i == 12:
                        sp.wait_ge(conv_done, g * 2 + 1)
                        sp.dma_start(t["y_conv"][:, bass.ds(g * 2, 1)], conv_y[:, 0:1, :]).then_inc(y_free[0], 16)
                        sp.wait_ge(u_ready, g * 4 + 4)
                        sp.dma_start(t["pool_p"][:, bass.ds(g * 2, 2)], pool_u[:, :, 1 + SEQ:POOL_MAX + SEQ]).then_inc(pool_state_stored, 16)
                        sp.dma_start(t["pool_s"][:, bass.ds(g * 2, 2)], ext_pool[:, :, 1:POOL_MAX, :]).then_inc(pool_state_stored, 16)
                sp.wait_ge(conv_done, g * 2 + 2)
                sp.dma_start(t["y_conv"][:, bass.ds(g * 2 + 1, 1)], conv_y[:, 1:2, :]).then_inc(y_free[1], 16)

            def load_main(s):
                sp.wait_ge(w_lo_done, s - 1)
                sp.dma_start(w_raw[:, s % 2, :], t["w_main"][s - PAIR_TOTAL + PAIRS * MAIN_PER_PAIR]).then_inc(raw_full[s % 2], 16)

            load_main(JOB_B + 2)
            for n in range(4):
                sp.wait_ge(b_lo_done, 2 * n + 2)
                if n == 0:
                    for x in range(2):
                        sp.wait_ge(y_free[x], 16 * (PAIRS + 1))
                sp.dma_start(bf[:, 2 * n:2 * n + 2, :], t["y_conv"][:, 2 * n:2 * n + 2]).then_inc(y_loaded[n], 16)
            load_main(JOB_B + 3)
            sp.wait_ge(pe_done, PAIR_TOTAL)
            for k in range(4):
                sp.wait_ge(stage_free[k], 16 * (PAIRS if k < 2 else 2 * PAIRS + 1))
            for n in range(4):
                rows = slice(2 * n, 2 * n + 2)
                sp.dma_start(hf[:, KT + 2 * n:KT + 2 * n + 2, :], t["sig_b"][:, rows]).then_inc(sigb_loaded[n], 16)
            load_main(JOB_B + 4)
            load_main(JOB_B + 5)
            sp.wait_ge(y_sq_summed, KT - 1)
            sp.dma_start(hf[:, 0:KT, :], t["silu_z"]).then_inc(siluz_loaded, 16)
            for s in range(JOB_B + 6, JOB_A + 2):
                load_main(s)
            sp.wait_ge(pe_done, JOB_A)
            sp.dma_start(gf[:, KT:KT + 2, :], t["sig_a"][:, 0:2]).then_inc(siga_loaded[0], 16)
            sp.dma_start(gate_raw[:], t["w_ada"][4]).then_inc(gate_loaded, 16)
            load_main(JOB_A + 2)
            sp.dma_start(gf[:, KT + 2:2 * KT, :], t["sig_a"][:, 2:KT]).then_inc(siga_loaded[1], 16)
            load_main(JOB_A + 3)
            load_main(JOB_A + 4)
            sp.wait_ge(gate_done, 1)
            sp.dma_start(gate_raw[:], t["w_ada"][5]).then_inc(gate_loaded, 16)
            for s in range(JOB_A + 5, JOB_OUT + 3):
                load_main(s)
            sp.wait_ge(pe_done, JOB_OUT)
            sp.dma_start(hf[:, 0:2, :], t["x_t"][:, 0:2]).then_inc(xres_loaded[0], 16)
            load_main(JOB_OUT + 3)
            sp.dma_start(hf[:, 2:KT, :], t["x_t"][:, 2:KT]).then_inc(xres_loaded[1], 16)
            for s in range(JOB_OUT + 4, JOBS):
                load_main(s)
            for c, m0, m1 in OUT_STORES:
                sp.wait_ge(y_out_ready, KT * c + m1)
                sp.dma_start(t["y"][:, m0:m1, cols(c)], hf[:, KT + m0:KT + m1, cols(c)]).then_inc(out_stored, 16)
            sp.wait_ge(out_stored, 16 * len(OUT_STORES))
            sp.wait_ge(conv_state_stored, 32 * (PAIRS + 1))
            sp.wait_ge(pool_state_stored, 32 * (PAIRS + 1))

        @block.gpsimd
        def _(pool):
            nc.gpsimd.memset(c_act[:], 0.0).then_inc(c_padded, 1)
            nc.gpsimd.memset(ones[:], 1.0 / D)
            nc.gpsimd.memset(eps[:, 0:1], RMS_EPS)
            nc.gpsimd.memset(row_mean[:], 0.0)
            nc.gpsimd.memset(eps[:, 1:2], LN_EPS).then_inc(ones_ready, 1)
            pool.wait_ge(ada_done, 4)
            nc.gpsimd.memset(conv_u[:, :, 0:CONV_BUF], 0.0)
            nc.gpsimd.memset(pool_u[:, :, 0:POOL_MAX], 0.0)
            nc.gpsimd.memset(pool_s[:, :, 0:POOL_MAX], 0.0).then_inc(pads_ready, 1)

        @block.tensor
        def _(pe):
            def modulation_product(bank, k, w):
                quad = slice(k % QUADS * QUAD, (k % QUADS + 1) * QUAD)
                return nc.tensor.matmul(bank[quad, :], c_act[:, k, :], w[:, k, :], start=(k < QUADS), stop=(k >= KT - QUADS),
                                        tile_position=(0, k % QUADS * QUAD))

            def modulation_turn(bank, rows):
                for j in range(ADA_BLOCKS):
                    last = nc.tensor.matmul(bank[:, j * NMOD:(j + 1) * NMOD], rows[:, j * P:(j + 1) * P], pick[:], start=True, stop=True)
                return last

            def keep_warm(n):
                for _ in range(n):
                    nc.tensor.matmul(ps[:, 0, 0, 0:P], ones[:], ones[:], start=True, stop=True)

            def ada(q):
                if q == 0:
                    pe.wait_ge(c_ready, 1)
                if q >= 2:
                    pe.wait_ge(x_std_ready, 4 - q)
                for k in range(KT):
                    if k % (KT // 2) == 0:
                        keep_warm(WARM_ADA[q][k // (KT // 2)])
                        pe.wait_ge(ada_loaded[q][k // (KT // 2)], 16)
                    last = modulation_product(ada_bank[q], k, ada_raw[:, q, :, :])
                last.then_inc(ada_done, 1)

            def turn(q):
                keep_warm(WARM_TURN[q])
                pe.wait_ge(ada_rows_ready, q + 1)
                modulation_turn(ada_bank[q], ada_rows[:, q % 2, :]).then_inc(ada_turned, 1)

            def token_sums(out, row, done):
                nc.tensor.matmul(out, ones[:], row, start=True, stop=True).then_inc(done, 1)

            pe.wait_ge(ones_ready, 1)
            pe.wait_ge(x_squared, KT - 2)
            keep_warm(WARM_SUMS)
            pe.wait_ge(x_summed, 1)
            token_sums(aux[:, 0, 0:CW], sq_sum[:, cols(0)], x_var_done)
            token_sums(aux[:, 1, 0:CW], sq_sum[:, cols(1)], x_var_done)
            token_sums(ps[:, 1, 1, 0:CW], sq_sum[:, cols(2)], x_var_done)
            def k_step(s_par, k, w_cols, rhs_hi, rhs_lo, n_k, chunks=range(CHUNKS)):
                wh = w_hi[:, s_par, w_cols]
                wl = w_lo[:, s_par, w_cols]
                for c in chunks:
                    out = ps[:, s_par, c, 0:CW]
                    nc.tensor.matmul(out, wh, rhs_hi[:, cols(c)], start=(k == 0), stop=False)
                    nc.tensor.matmul(out, wh, rhs_lo[:, cols(c)], start=False, stop=False)
                for c in chunks:
                    last = nc.tensor.matmul(ps[:, s_par, c, 0:CW], wl, rhs_hi[:, cols(c)], start=False, stop=(k == n_k - 1))
                return last

            def h_step(i, k):
                return k_step(i % 2, k, slice(k * P, (k + 1) * P), hr[:, k, :], hr[:, KT + k, :], KT)

            def pair_job(g, i):
                kind, tile, _ = PAIR_JOBS[i]
                pe.wait_ge(w_lo_done, g * JOBS_PER_PAIR + (i + 1))
                if i < 2:
                    pe.wait_ge(act_evac, g * ACT_EVACS + (i + 1))
                elif PAIR_JOBS[i - 2][2] == "act":
                    pe.wait_ge(act_evac, g * ACT_EVACS + (2 + evacs("act", i - 2)))
                else:
                    pe.wait_ge(dve_evac, g * DVE_EVACS + evacs("dve", i - 2))
                if kind == "pool_mix":
                    if tile == 0:
                        pe.wait_ge(p_lo_done, g * 2 + 2)
                    for k in range(2):
                        last = k_step(i % 2, k, slice(k * P, (k + 1) * P), pool_p[:, k, :], pool_p[:, 2 + k, :], 2)
                else:
                    for k in range(KT):
                        last = h_step(i, k)
                last.then_inc(pe_done, 1)

            together = KT - 2

            def side_by_side(k):
                if k == 0:
                    pe.wait_ge(w_lo_done, 2)
                    pe.wait_ge(ada_mod_done, 2)
                    pe.wait_ge(x_std_ready, CHUNKS)
                pe.wait_ge(h_lo_done, k + 1)
                h_step(0, k)
                h_step(1, k)

            for q in range(2):
                ada(q)
                turn(q)
            for q in range(2, 4):
                ada(q)
                side_by_side(q - 2)
                turn(q)
            for k in range(2, together):
                side_by_side(k)
            for i in range(2):
                for k in range(together, KT):
                    if i == 0:
                        pe.wait_ge(h_lo_done, k + 1)
                    last = h_step(i, k)
                last.then_inc(pe_done, 1)
            for i in range(2, JOBS_PER_PAIR):
                pair_job(0, i)
            with pe.Fori(1, PAIRS) as g:
                for i in range(JOBS_PER_PAIR):
                    pair_job(g, i)

            def job(s_par, hi, lo, after_k=None, before_k=None):
                for k in range(KT):
                    if before_k:
                        before_k(k)
                    last = k_step(s_par, k, slice(k * P, (k + 1) * P), hi[k], lo[k], KT)
                    if after_k:
                        after_k(k)
                last.then_inc(pe_done, 1)

            b_hi = [gr[:, k, :] for k in range(KT)]
            b_lo = [gr[:, KT + k, :] for k in range(KT)]

            def mean_third(k):
                if k == 3:
                    pe.wait_ge(mean_ready, 1)
                    token_sums(aux[:, 0, 0:CW], row_mean[:, cols(2)], mean_done)

            def var_sums(k):
                if k == 2:
                    pe.wait_ge(y_sq_summed, KT - 1)
                    pe.wait_ge(mean_ready, CHUNKS)
                    for c in range(2):
                        token_sums(aux[:, c, 0:CW], sq_sum[:, cols(c)], y_var_done)
                if k == 4:
                    pe.wait_ge(y_std_ready, 1)
                    token_sums(aux[:, 0, 0:CW], sq_sum[:, cols(2)], y_var_done)

            def job_pairs(first, count, hi, lo):
                with pe.Fori(0, count // 2) as r:
                    for par_ in range(2):
                        pe.wait_ge(w_lo_done, r * 2 + (first + par_ + 1))
                        pe.wait_ge(dve_evac, r * 2 + (PAIRS * DVE_EVACS + first + par_ - 1 - JOB_B))
                        job((first + par_) % 2, hi, lo)

            pe.wait_ge(y_summed, 2 * PAIRS)
            for c in range(2):
                token_sums(aux[:, c, 0:CW], row_mean[:, cols(c)], mean_done)
            for s in range(JOB_B, JOB_B + 4):
                pe.wait_ge(w_lo_done, s + 1)
                if s == JOB_B:
                    pe.wait_ge(dve_evac, PAIRS * DVE_EVACS)
                elif s == JOB_B + 1:
                    pe.wait_ge(act_evac, 2 + PAIRS * ACT_EVACS)
                else:
                    pe.wait_ge(dve_evac, PAIRS * DVE_EVACS + s - 1 - JOB_B)
                job(s % 2, b_hi, b_lo,
                    after_k={JOB_B: mean_third, JOB_B + 3: var_sums}.get(s),
                    before_k=(lambda k: pe.wait_ge(b_lo_done, k + 1)) if s == JOB_B else None)

            job_pairs(JOB_B + 4, 4, b_hi, b_lo)
            a_hi = [br[:, k, :] for k in range(KT)]
            a_lo = [hr[:, k, :] for k in range(KT)]

            def single(s, hi, lo, before_k=None):
                pe.wait_ge(w_lo_done, s + 1)
                pe.wait_ge(dve_evac, PAIRS * DVE_EVACS + s - 1 - JOB_B)
                job(s % 2, hi, lo, before_k=before_k)

            def gate_chunk(n):
                pe.wait_ge(gate_loaded, 16 * (n + 1))
                for k in range(KT):
                    last = modulation_product(aux[:, n, :], k, gate_raw)
                last.then_inc(gate_done, 1)

            def gate_turn(n):
                pe.wait_ge(gate_rows_ready, n + 1)
                modulation_turn(aux[:, n, :], gate_rows).then_inc(gate_turned, 1)

            single(JOB_A, a_hi, a_lo, before_k=lambda k: pe.wait_ge(a_lo_done, k + 1))
            job_pairs(JOB_A + 1, 2, a_hi, a_lo)
            gate_chunk(0)
            single(JOB_A + 3, a_hi, a_lo)
            gate_turn(0)
            gate_chunk(1)
            single(JOB_A + 4, a_hi, a_lo)
            gate_turn(1)
            single(JOB_A + 5, a_hi, a_lo)
            job_pairs(JOB_A + 6, 2, a_hi, a_lo)
            m_hi, m_lo = b_hi, b_lo
            single(JOB_OUT, m_hi, m_lo, before_k=lambda k: pe.wait_ge(m_lo_done, k + 1))
            job_pairs(JOB_OUT + 1, 4, m_hi, m_lo)
            single(JOB_OUT + 5, m_hi, m_lo)

            def final_var(c):
                pe.wait_ge(x_new_summed, c + 1)
                token_sums(aux[:, c % 2, 0:CW], sq_sum[:, cols(c)], f_var_done)

            for c in range(CHUNKS):
                for s in (JOBS - 2, JOBS - 1):
                    if c == 0:
                        pe.wait_ge(w_lo_done, s + 1)
                        pe.wait_ge(dve_evac, PAIRS * DVE_EVACS + s - 1 - JOB_B)
                    for k in range(KT):
                        last = k_step(s % 2, k, slice(k * P, (k + 1) * P), m_hi[k], m_lo[k], KT, chunks=[c])
                    if s == JOBS - 2 and c >= 1:
                        final_var(c - 1)
                last.then_inc(pe_done, 1)
            pe.wait_ge(x_new_ready, KT - 1)
            keep_warm(WARM_FINAL)
            pe.wait_ge(f_std_ready, 1)
            final_var(2)

        def weight_columns(i):
            return MIX_WIDTH if PAIR_JOBS[i % JOBS_PER_PAIR][0] == "pool_mix" else KT * P

        @block.scalar
        def _(act):
            def split_hi(slot, n, loaded):
                act.wait_ge(raw_full[slot], loaded)
                nc.scalar.activation(w_hi[:, slot, 0:n], w_raw[:, slot, 0:n], ACT.Copy).then_inc(w_hi_done, 1)

            act.sem_inc(act_evac, 2)
            act.sem_inc(stage_free[2], 16)
            act.sem_inc(stage_free[3], 16)
            act.sem_inc(y_free[0], 16)
            act.sem_inc(y_free[1], 16)
            act.sem_inc(conv_state_stored, 32)
            act.sem_inc(pool_state_stored, 32)

            act.wait_ge(small_loaded, 64)
            act.wait_ge(c_padded, 1)
            nc.scalar.activation(c_act[:, :, 0:NMOD], c_in[:], ACT.Silu).then_inc(c_ready, 1)

            def ada_out(q):
                act.wait_ge(ada_done, q + 1)
                if q >= 2:
                    act.wait_ge(ada_turned, q - 1)
                nc.scalar.activation(ada_rows[:, q % 2, :], ada_bank[q], ACT.Copy).then_inc(ada_rows_ready, 1)

            def h_hi(e):
                act.wait_ge(h_scaled, e + 1)
                nc.scalar.activation(bf[:, e, 0:SEQ], bf[:, e, 0:SEQ], ACT.Identity, bias=mod[:, e // 2, e % 2, 0:1]).then_inc(h_shifted, 1)
                act.wait_ge(h_shifted, e + 1)
                nc.scalar.activation(hr[:, e, :], bf[:, e, :], ACT.Copy).then_inc(h_hi_done, 1)

            for e in range(KT):
                act.wait_ge(x_loaded[e // 2], 16)
                nc.scalar.activation(hf[:, e, :], bf[:, e, :], ACT.Square).then_inc(x_squared, 1)
            for s in range(2):
                split_hi(s, KT * P, 16)
            for c in range(CHUNKS):
                src = ps[:, 1, 1, 0:CW] if c == 2 else aux[:, c, 0:CW]
                act.wait_ge(x_var_done, c + 1)
                nc.scalar.activation(row_rstd[:, cols(c)], src, ACT.Sqrt, bias=eps[:, 0:1]).then_inc(x_std_ready, 1)
            for q in range(4):
                ada_out(q)
                if q >= 1:
                    h_hi(2 * q - 2)
                    h_hi(2 * q - 1)
            h_hi(KT - 2)
            h_hi(KT - 1)
            STAGED = {4: (0, "sig_a"), 5: (1, "sig_a"), 6: (2, "sig_b"), 7: (3, "sig_b"), 13: (2, "silu_z"), 15: (3, "silu_z")}

            def pair_step(g, i):
                kind, tile, engine = PAIR_JOBS[i]
                act.wait_ge(pe_done, g * JOBS_PER_PAIR + (i + 1))
                raw_count = g * (JOBS_PER_PAIR // 2 * 16) + 16 * ((i + 2) // 2 + 1)
                if i in SHORT_NEXT:
                    split_hi(i % 2, weight_columns(i + 2), raw_count)
                if engine == "act":
                    src = ps_job(i)
                    if kind == "glu_gate":
                        if tile == 1:
                            act.wait_ge(dve_evac, g * DVE_EVACS + 1)
                        dst, func = sig[:], ACT.Sigmoid
                    elif kind in ("merge_a", "merge_b"):
                        slot = STAGED[i][0]
                        if slot >= 2:
                            act.wait_ge(stage_free[slot], g * 32 + 16)
                        dst, func = stage[slot], ACT.Sigmoid
                    elif kind == "pool_in":
                        if tile == 0:
                            act.wait_ge(pool_state_stored, g * 32 + 32)
                        dst, func = pool_u[:, tile, POOL_MAX:POOL_MAX + TOK], ACT.Copy
                    elif kind == "pool_z":
                        act.wait_ge(stage_free[tile], g * 16 + 16)
                        dst, func = stage[tile], ACT.Silu
                    else:
                        act.wait_ge(stage_free[2 + tile], g * 32 + 32)
                        dst, func = stage[2 + tile], ACT.Silu
                    nc.scalar.activation(by_chunk(dst), src, func).then_inc(act_evac, 1)
                if i not in SHORT_NEXT:
                    split_hi(i % 2, weight_columns(i + 2), raw_count)
                if i in STAGED:
                    slot, name = STAGED[i]
                    act.wait_ge(act_evac, g * ACT_EVACS + (2 + evacs("act", i)))
                    act.dma_start(t[name][:, bass.ds(g * 2 + tile, 1)] if not isinstance(g, int) else t[name][:, 2 * g + tile:2 * g + tile + 1],
                                  stage[slot].rearrange("p (a t) -> p a t", a=1)).then_inc(stage_free[slot], 16)
                if i in (8, 9):
                    act.wait_ge(p_ready, g * 2 + (i - 7))
                    nc.scalar.activation(pool_p[:, tile, :], sig[:], ACT.Copy).then_inc(p_hi_done, 1)

            with act.Fori(0, PAIRS - 1) as g:
                for i in range(JOBS_PER_PAIR):
                    pair_step(g, i)
            for i in range(JOBS_PER_PAIR - 1):
                pair_step(PAIRS - 1, i)
            for e in range(KT):
                if e == 0:
                    act.wait_ge(dve_evac, PAIRS * DVE_EVACS)
                    act.wait_ge(y_free[0], 16 * (PAIRS + 1))
                    act.wait_ge(y_free[1], 16 * (PAIRS + 1))
                    act.wait_ge(conv_state_stored, 32 * (PAIRS + 1))
                    act.wait_ge(pool_state_stored, 32 * (PAIRS + 1))
                    act.wait_ge(p_lo_done, 2 * PAIRS)
                    act.wait_ge(y_summed, 2 * PAIRS)
                nc.scalar.activation(gr[:, e, :], bf[:, e, :], ACT.Copy).then_inc(b_hi_done, 1)
            pair_step(PAIRS - 1, JOBS_PER_PAIR - 1)

            def split_for(s):
                if s + 2 < JOBS:
                    act.wait_ge(pe_done, s + 1)
                    split_hi(s % 2, KT * P, 16 * ((s + 2) // 2 + 1))

            for c in range(CHUNKS):
                act.wait_ge(mean_done, c + 1)
                nc.scalar.activation(row_mean[:, cols(c)], aux[:, c % 2, 0:CW], ACT.Copy).then_inc(mean_ready, 1)
            for e in range(KT):
                if e == 4:
                    split_for(JOB_B)
                act.wait_ge(y_centred, e + 1)
                nc.scalar.activation(hf[:, e, :], bf[:, e, :], ACT.Square).then_inc(y_squared, 1)
            split_for(JOB_B + 1)
            split_for(JOB_B + 2)
            for c in range(CHUNKS):
                act.wait_ge(y_var_done, c + 1)
                nc.scalar.activation(row_rstd[:, cols(c)], aux[:, c % 2, 0:CW], ACT.Sqrt, bias=eps[:, 1:2]).then_inc(y_std_ready, 1)

            def silu_y(e):
                act.wait_ge(y_normed, e + 1)
                nc.scalar.activation(bf[:, e, :], bf[:, e, :], ACT.Silu, bias=vecs[:, LN_B, e:e + 1],
                                     scale=vecs[:, LN_G, e:e + 1]).then_inc(y_silu, 1)

            silu_y(0)
            silu_y(1)
            split_for(JOB_B + 3)
            for e in range(KT):
                act.wait_ge(a_full, e + 1)
                nc.scalar.activation(br[:, e, :], full_a, ACT.Copy).then_inc(a_hi_done, 1)
                if e in (1, 3, 5):
                    split_for(JOB_B + 4 + e // 2)
                if e + 2 < KT:
                    silu_y(e + 2)
            split_for(JOB_B + 7)
            for m in range(KT):
                if m in (3, 4):
                    n = m - 3
                    act.wait_ge(gate_done, n + 1)
                    nc.scalar.activation(gate_rows[:], aux[:, n, :], ACT.Copy).then_inc(gate_rows_ready, 1)
                split_for(JOB_A + m)
                act.wait_ge(m_full, m + 1)
                nc.scalar.activation(gr[:, m, :], hf[:, KT + m, :], ACT.Copy).then_inc(m_hi_done, 1)
            for m in range(KT - 2):
                split_for(JOB_OUT + m)
                act.wait_ge(x_new_ready, m + 1)
                nc.scalar.activation(bf[:, m, :], hf[:, KT + m, :], ACT.Square).then_inc(x_new_squared, 1)

            def last_squares(c):
                act.wait_ge(x_new_ready, KT - 1 + c)
                nc.scalar.activation(bf[:, KT - 2:KT, cols(c)], hf[:, 2 * KT - 2:2 * KT, cols(c)], ACT.Square).then_inc(x_new_squared, 1)

            last_squares(0)
            for c in range(CHUNKS):
                act.wait_ge(f_var_done, c + 1)
                nc.scalar.activation(row_rstd[:, cols(c)], aux[:, c % 2, 0:CW], ACT.Sqrt, bias=eps[:, 0:1]).then_inc(f_std_ready, 1)
                if c + 1 < CHUNKS:
                    last_squares(c + 1)

        @block.vector
        def _(dve):
            v = nc.vector
            links = [0]
            at_pair = [None]

            def link(ins):
                links[0] += 1
                ins.then_inc(dve_chain, 1)
                g = at_pair[0]
                dve.wait_ge(dve_chain, links[0] if g is None else g * LINKS + links[0])

            def split_lo(slot, n, count):
                dve.wait_ge(w_hi_done, count)
                v.tensor_tensor(w_lo[:, slot, 0:n], w_raw[:, slot, 0:n], w_hi[:, slot, 0:n].bitcast(F32), ALU.subtract).then_inc(w_lo_done, 1)

            def wide(ap, n):
                return ap.unsqueeze(2).broadcast_to([P, ap.shape[1], n])

            for e in range(1, KT):
                dve.wait_ge(x_squared, e + 1)
                link(v.tensor_tensor(sq_sum, hf[:, 0, :] if e == 1 else sq_sum, hf[:, e, :], ALU.add))
            dve.sem_inc(x_summed, 1)

            def modulation(q):
                dve.wait_ge(ada_turned, q + 1)
                link(v.tensor_tensor(mod[:, q, :, :], ada_bank[q][:, 0:ADA_BLOCKS * NMOD].rearrange("p (j n) -> p j n", j=ADA_BLOCKS),
                                     wide(ada_b[:, q, :], NMOD), ALU.add))
                link(v.scalar_tensor_tensor(out=mod[:, q, 2:4, :], in0=mod[:, q, 2:4, :], scalar=1.0,
                                                in1=wide(vecs[:, G_NORM, 2 * q:2 * q + 2], NMOD), op0=ALU.add, op1=ALU.mult))
                dve.sem_inc(ada_mod_done, 1)

            split_lo(0, KT * P, 1)
            dve.wait_ge(small_loaded, 64)
            for c in range(CHUNKS):
                dve.wait_ge(x_std_ready, c + 1)
                link(v.reciprocal(row_rstd[:, cols(c)], row_rstd[:, cols(c)]))

            def h_samples(q):
                xs = bf[:, 2 * q:2 * q + 2, SEQ:TOK]
                link(v.tensor_tensor(xs, xs, mod[:, q, 2:4, 1:NMOD], ALU.mult))
                link(v.tensor_tensor(xs, xs, row_rstd[:, SEQ:TOK].unsqueeze(1).broadcast_to([P, 2, NSAMP]), ALU.mult))
                v.tensor_tensor(xs, xs, mod[:, q, 0:2, 1:NMOD], ALU.add)

            def h_tile(e):
                q, j = e // 2, e % 2
                xp = bf[:, e, 0:SEQ]
                v.scalar_tensor_tensor(out=xp, in0=xp, scalar=mod[:, q, 2 + j, 0:1], in1=row_rstd[:, 0:SEQ], op0=ALU.mult, op1=ALU.mult).then_inc(h_scaled, 1)

            def h_lo(e):
                dve.wait_ge(h_hi_done, e + 1)
                v.tensor_tensor(hr[:, KT + e, :], bf[:, e, :], hr[:, e, :].bitcast(F32), ALU.subtract).then_inc(h_lo_done, 1)

            for q in range(4):
                modulation(q)
                h_samples(q)
                h_tile(2 * q)
                if q >= 1:
                    h_lo(2 * q - 1)
                h_tile(2 * q + 1)
                if q == 0:
                    split_lo(1, KT * P, 2)
                h_lo(2 * q)
            h_lo(KT - 1)
            dve.wait_ge(pads_ready, 1)
            dve.wait_ge(par_loaded, 32)

            base_links = links[0]
            LEVELS = [pool_u, pool_s]

            def tap(x, k):
                y = conv_y[:, x, 0:SEQ]
                if k == 0:
                    return v.tensor_scalar(y, conv_u[:, x, 0:SEQ], par[:, x, 0:1], par[:, x, CONV_W:CONV_W + 1], ALU.mult, ALU.add)
                return v.scalar_tensor_tensor(out=y, in0=conv_u[:, x, k:k + SEQ], scalar=par[:, x, k:k + 1], in1=y, op0=ALU.mult, op1=ALU.add)

            def conv_samples(g, x):
                if x == 0:
                    dve.wait_ge(ext_loaded, g * 32 + 32)
                ys = conv_y[:, x, SEQ:TOK]
                link(v.tensor_tensor(prod[:], ext_conv[:, x, :, :], wide(par[:, x, 0:CONV_W], NSAMP), ALU.mult))
                link(v.tensor_reduce(ys, prod[:].rearrange("p k s -> p s k"), AX_X, ALU.add))
                v.tensor_scalar(ys, ys, par[:, x, CONV_W:CONV_W + 1], None, ALU.add)

            def taps(g, n):
                for _ in range(n):
                    x, k = divmod(tap_at[0], CONV_W)
                    if k == 0:
                        dve.wait_ge(y_free[x], g * 16 + 16)
                        conv_samples(g, x)
                    link(tap(x, k))
                    if k == CONV_W - 1:
                        v.tensor_tensor(row_mean[:], row_mean[:], conv_y[:, x, :], ALU.add).then_inc(y_summed, 1)
                        dve.sem_inc(conv_done, 1)
                    tap_at[0] += 1

            def pool_tile(g, x, split):
                u = pool_u[:, x, :]
                levels = [u, pool_s[:, 0, :], pool_s[:, 1, :], pool_s[:, 0, :], pool_s[:, 1, :]]
                for n in range(DOUBLINGS):
                    src, dst = levels[n], levels[n + 1]
                    back = 1 << n
                    link(v.scalar_tensor_tensor(out=dst[:, POOL_MAX:POOL_MAX + SEQ], in0=src[:, POOL_MAX - back:POOL_MAX + SEQ - back],
                                                scalar=poolc[:, n:n + 1], in1=src[:, POOL_MAX:POOL_MAX + SEQ], op0=ALU.mult, op1=ALU.add))
                    if n == 0:
                        split()
                full = sig[:]
                sums = levels[DOUBLINGS]
                v.scalar_tensor_tensor(out=full[:, POOL_MAX:SEQ], in0=sums[:, 2 * POOL_MAX:POOL_MAX + SEQ], scalar=poolc[:, DOUBLINGS:DOUBLINGS + 1],
                                       in1=u[:, 2 * POOL_MAX:POOL_MAX + SEQ], op0=ALU.mult, op1=ALU.subtract)
                inv = poolc[:, DOUBLINGS + 1:DOUBLINGS + 1 + POOL_MAX]
                v.tensor_tensor(full[:, 0:POOL_MAX], sums[:, POOL_MAX:2 * POOL_MAX], inv, ALU.mult)
                win = poolc[:, DOUBLINGS + 1 + POOL_MAX:N_POOLC]
                link(v.tensor_tensor(prod[:, 0:POOL_MAX, :], ext_pool[:, x, :, :], wide(win, NSAMP), ALU.mult))
                link(v.tensor_reduce(full[:, SEQ:TOK], prod[:, 0:POOL_MAX, :].rearrange("p k s -> p s k"), AX_X, ALU.add))
                v.tensor_tensor(full[:, 0:POOL_MAX], full[:, 0:POOL_MAX], u[:, POOL_MAX:2 * POOL_MAX], ALU.subtract)
                v.tensor_tensor(full[:, SEQ:TOK], full[:, SEQ:TOK], u[:, POOL_MAX + SEQ:POOL_MAX + TOK], ALU.subtract).then_inc(p_ready, 1)

            def pool_lo(g, x):
                dve.wait_ge(p_hi_done, g * 2 + (x + 1))
                link(v.tensor_tensor(pool_p[:, 2 + x, :], sig[:], pool_p[:, x, :].bitcast(F32), ALU.subtract))
                dve.sem_inc(p_lo_done, 1)

            tap_at = [0]

            def pair_step(g, i):
                kind, tile, engine = PAIR_JOBS[i]
                dve.wait_ge(pe_done, g * JOBS_PER_PAIR + (i + 1))
                if i == 0:
                    tap_at[0] = 0
                    if isinstance(g, int):
                        v.tensor_copy(par[:], par_all[:, g, :, :])
                        link(v.tensor_copy(poolc[:], poolc_all[:, g, :]))
                    else:
                        v.tensor_copy(par[:], par_all[:, bass.ds(g, 1), :, :].rearrange("p a x n -> p (a x) n"))
                        link(v.tensor_copy(poolc[:], poolc_all[:, bass.ds(g, 1), :].rearrange("p a n -> p (a n)")))
                if kind == "glu_value":
                    dve.wait_ge(act_evac, g * ACT_EVACS + (2 + evacs("act", i - 1)))
                    if tile == 0:
                        dve.wait_ge(conv_state_stored, g * 32 + 32)
                        dve.wait_ge(ext_loaded, g * 32 + 32)
                    link(v.tensor_tensor(by_chunk(conv_u[:, tile, CONV_BUF:CONV_BUF + TOK]), ps_job(i), by_chunk(sig[:]), ALU.mult))
                    dve.sem_inc(dve_evac, 1)
                    v.tensor_copy(ext_conv[:, tile, CONV_BUF, :], conv_u[:, tile, CONV_BUF + SEQ:CONV_BUF + TOK]).then_inc(u_ready, 1)
                    dve.wait_ge(u_ready, g * 4 + (tile + 1))
                if kind == "pool_mix":
                    dve.wait_ge(act_evac, g * ACT_EVACS + (2 + evacs("act", 10 + tile)))
                    e = g * 2 + tile
                    dst = bf[:, e, :] if isinstance(g, int) else bf[:, bass.ds(e, 1), :].rearrange("p a t -> p (a t)")
                    v.scalar_tensor_tensor(out=by_chunk(dst), in0=ps_job(i), scalar=par[:, tile, CONV_W + 1:CONV_W + 2],
                                           in1=by_chunk(stage[tile]), op0=ALU.mult, op1=ALU.mult).then_inc(dve_evac, 1)
                def split():
                    split_lo(i % 2, weight_columns(i + 2), g * JOBS_PER_PAIR + (i + 3))

                before, after = (LAST_TAPS_AT if isinstance(g, int) else TAPS_AT).get(i, (0, 0))
                taps(g, before)
                if i in (8, 9):
                    dve.wait_ge(act_evac, g * ACT_EVACS + (2 + evacs("act", i)))
                    if tile == 1:
                        pool_lo(g, 0)
                    v.tensor_copy(ext_pool[:, tile, POOL_BUF, :], pool_u[:, tile, POOL_MAX + SEQ:POOL_MAX + TOK]).then_inc(u_ready, 1)
                    pool_tile(g, tile, split)
                if i == 10:
                    pool_lo(g, 1)
                if i not in (8, 9):
                    split()
                taps(g, after)

            with dve.Fori(0, PAIRS - 1) as g:
                at_pair[0] = g
                for i in range(JOBS_PER_PAIR):
                    pair_step(g, i)
                assert links[0] - base_links == LINKS, (links[0] - base_links, LINKS)
            at_pair[0] = None
            links[0] = base_links + (PAIRS - 1) * LINKS
            for i in range(JOBS_PER_PAIR - 1):
                pair_step(PAIRS - 1, i)
            for e in range(KT):
                dve.wait_ge(b_hi_done, e + 1)
                v.tensor_tensor(gr[:, KT + e, :], bf[:, e, :], gr[:, e, :].bitcast(F32), ALU.subtract).then_inc(b_lo_done, 1)
            pair_step(PAIRS - 1, JOBS_PER_PAIR - 1)

            def split_for(s):
                if s + 2 < JOBS:
                    split_lo(s % 2, KT * P, s + 3)

            def merge_b(m):
                s = JOB_B + m
                dve.wait_ge(pe_done, s + 1)
                dve.wait_ge(sigb_loaded[m // 2], 16)
                row = hf[:, KT + m, :]
                v.tensor_tensor(by_chunk(row), ps_job(s), by_chunk(row), ALU.mult).then_inc(dve_evac, 1)

            dve.wait_ge(mean_ready, CHUNKS)
            for e in range(KT):
                dve.wait_ge(y_loaded[e // 2], 16)
                v.tensor_tensor(bf[:, e, :], bf[:, e, :], row_mean[:], ALU.subtract).then_inc(y_centred, 1)
                if e == 5:
                    merge_b(0)
                    split_for(JOB_B)
            for e in range(1, KT):
                dve.wait_ge(y_squared, e + 1)
                v.tensor_tensor(sq_sum, hf[:, 0, :] if e == 1 else sq_sum, hf[:, e, :], ALU.add).then_inc(y_sq_summed, 1)
                dve.wait_ge(y_sq_summed, e)
            merge_b(1)
            split_for(JOB_B + 1)
            merge_b(2)
            split_for(JOB_B + 2)
            for c in range(CHUNKS):
                dve.wait_ge(y_std_ready, c + 1)
                link(v.reciprocal(row_rstd[:, cols(c)], row_rstd[:, cols(c)]))
            for e in range(KT):
                if e == 3:
                    merge_b(3)
                    split_for(JOB_B + 3)
                last = v.tensor_tensor(bf[:, e, :], bf[:, e, :], row_rstd, ALU.mult)
                last.then_inc(y_normed, 1)
            dve.wait_ge(siluz_loaded, 16)
            dve.wait_ge(y_normed, KT)
            for e in range(KT):
                dve.wait_ge(y_silu, e + 1)
                v.tensor_tensor(full_a, bf[:, e, :], hf[:, e, :], ALU.mult).then_inc(a_full, 1)
                if e in (1, 3, 5):
                    merge_b(4 + e // 2)
                    split_for(JOB_B + 4 + e // 2)
                dve.wait_ge(a_hi_done, e + 1)
                link(v.tensor_tensor(hr[:, e, :], full_a, br[:, e, :].bitcast(F32), ALU.subtract))
                dve.sem_inc(a_lo_done, 1)
            merge_b(7)
            split_for(JOB_B + 7)

            for m in range(KT):
                s = JOB_A + m
                dve.wait_ge(pe_done, s + 1)
                dve.wait_ge(siga_loaded[min(m // 2, 1)], 16)
                t_row, m_row = gf[:, KT + m, :], hf[:, KT + m, :]
                v.tensor_tensor(by_chunk(t_row), ps_job(s), by_chunk(t_row), ALU.mult).then_inc(dve_evac, 1)
                dve.wait_ge(dve_evac, PAIRS * DVE_EVACS + s + 1 - JOB_B)
                v.tensor_tensor(m_row, t_row, m_row, ALU.add).then_inc(m_full, 1)
                split_for(s)
                dve.wait_ge(m_hi_done, m + 1)
                v.tensor_tensor(gr[:, KT + m, :], m_row, gr[:, m, :].bitcast(F32), ALU.subtract).then_inc(m_lo_done, 1)
                if m in (4, 5):
                    n = m - 4
                    dve.wait_ge(gate_turned, n + 1)
                    v.tensor_tensor(mod[:, 4 + n, :, :], aux[:, n, 0:ADA_BLOCKS * NMOD].rearrange("p (j n) -> p j n", j=ADA_BLOCKS),
                                    wide(ada_b[:, 4 + n, :], NMOD), ALU.add).then_inc(gate_ready, 1)

            def new_x(m, c0, c1):
                gate = mod[:, 4 + m // 4, m % 4, :]
                hi = min(c1 * CW, SEQ)
                for c in range(c0, c1):
                    w = min(CW, SEQ - c * CW)
                    last = v.scalar_tensor_tensor(out=hf[:, KT + m, c * CW:c * CW + w], in0=ps[:, (JOB_OUT + m) % 2, c, 0:w],
                                                  scalar=gate[:, 0:1], in1=hf[:, m, c * CW:c * CW + w], op0=ALU.mult, op1=ALU.add)
                if c1 == CHUNKS:
                    xs = hf[:, KT + m, SEQ:TOK]
                    link(v.tensor_tensor(xs, ps[:, (JOB_OUT + m) % 2, CHUNKS - 1, CW - NSAMP:CW], gate[:, 1:NMOD], ALU.mult))
                    last = v.tensor_tensor(xs, xs, hf[:, m, SEQ:TOK], ALU.add)
                return last

            dve.wait_ge(gate_ready, 2)
            for m in range(KT - 2):
                dve.wait_ge(pe_done, JOB_OUT + m + 1)
                dve.wait_ge(xres_loaded[min(m // 2, 1)], 16)
                link(new_x(m, 0, CHUNKS))
                dve.sem_inc(dve_evac, 1)
                dve.sem_inc(x_new_ready, 1)
                split_for(JOB_OUT + m)
                if m >= 1:
                    dve.wait_ge(x_new_squared, m + 1)
                    link(v.tensor_tensor(sq_sum, bf[:, 0, :] if m == 1 else sq_sum, bf[:, m, :], ALU.add))

            def last_x(c):
                dve.wait_ge(pe_done, JOBS - 1 + c)
                new_x(KT - 2, c, c + 1)
                new_x(KT - 1, c, c + 1).then_inc(x_new_ready, 1)

            def last_sum(c):
                dve.wait_ge(x_new_squared, KT - 1 + c)
                link(v.tensor_tensor(sq_sum[:, cols(c)], sq_sum[:, cols(c)], bf[:, KT - 2, cols(c)], ALU.add))
                v.tensor_tensor(sq_sum[:, cols(c)], sq_sum[:, cols(c)], bf[:, KT - 1, cols(c)], ALU.add).then_inc(x_new_summed, 1)

            def inverse(c):
                dve.wait_ge(f_std_ready, c + 1)
                link(v.reciprocal(row_rstd[:, cols(c)], row_rstd[:, cols(c)]))

            def norm(c, tiles):
                for m in tiles:
                    row = hf[:, KT + m, cols(c)]
                    v.scalar_tensor_tensor(out=row, in0=row, scalar=vecs[:, G_FINAL, m:m + 1], in1=row_rstd[:, cols(c)],
                                           op0=ALU.mult, op1=ALU.mult).then_inc(y_out_ready, 1)

            last_x(0)
            last_sum(0)
            for c in range(CHUNKS - 1):
                inverse(c)
                last_x(c + 1)
                norm(c, range(KT // 2))
                last_sum(c + 1)
                norm(c, range(KT // 2, KT))
            inverse(CHUNKS - 1)
            norm(CHUNKS - 1, range(KT))


def kernel(**inputs):
    import numpy as np
    import concourse.bacc as bacc
    from concourse.bass_utils import run_bass_kernel_spmd

    a = {k: np.asarray(v) for k, v in inputs.items()}
    cat = np.concatenate

    def channel_major(x):
        return x.T.reshape(KT, P, -1).transpose(1, 0, 2)

    def column_blocks(w, width=P):
        k, n = w.shape
        return w.reshape(k // P, P, n // width, width).transpose(2, 1, 0, 3).reshape(n // width, P, -1)

    w_in = {kind: column_blocks(a["w_in"][0][:, part * D:(part + 1) * D]) for kind, part in W_IN_PART.items()}
    main = [w_in[kind][2 * g + tile] for g in range(PAIRS) for kind, tile, _ in PAIR_JOBS if kind != "pool_mix"]
    main = cat([np.stack(main), column_blocks(a["w_b_out"][0]), column_blocks(a["w_a_out"][0]), column_blocks(a["w_out"][0])])
    mix = cat([column_blocks(a["w_grp"][0][g]) for g in range(PAIRS)])

    w_ada, b_ada = a["w_ada"][0], a["b_ada"][0]
    order = [np.arange(part * D + 2 * q * P, part * D + (2 * q + 2) * P) for q in range(PAIRS) for part in (0, 1)]
    order = cat(order + [np.arange(2 * D, 3 * D)])
    ada = column_blocks(w_ada[:, order], ADA_CHUNK).reshape(6, P, KT, ADA_CHUNK)
    ada_b = b_ada[order].reshape(6, ADA_BLOCKS, P).transpose(2, 0, 1)

    def column(x):
        return x.reshape(KT, P).T

    par = cat([a["w_dw"][0], a["b_dw"], a["pool_scale"]])
    par = channel_major(par).reshape(P, PAIRS, 2, N_PAR)
    poolc = np.zeros((P, PAIRS, N_POOLC), np.float32)
    for g in range(PAIRS):
        w = 2 << g
        poolc[:, g, 0:g + 1] = 1.0
        poolc[:, g, DOUBLINGS] = 1.0 / w
        poolc[:, g, DOUBLINGS + 1:DOUBLINGS + 1 + POOL_MAX] = 1.0 / np.minimum(np.arange(POOL_MAX) + 1, w)
        poolc[:, g, N_POOLC - w:] = 1.0 / w

    def state(x):
        return x.transpose(2, 1, 0).reshape(KT, P, x.shape[1], NSAMP).transpose(1, 0, 2, 3)

    sent = {
        "x_t": channel_major(cat([a["x_prompt"][0], a["x_sample"][:, 0]])),
        "c_t": channel_major(cat([a["c_prompt"], a["c_sample"]])),
        "pick": np.tile(np.eye(QUAD, NMOD, dtype=np.float32), (QUADS, 1)),
        "w_ada": ada, "ada_b": ada_b, "w_main": main, "w_mix": mix,
        "vecs": np.stack([column(a["g_norm"][0]), column(a["ln_g"][0]), column(a["ln_b"][0]), column(a["g_final"])], 1),
        "par": par, "poolc": poolc,
        "state_conv": state(a["state_conv"][0]), "state_pool": state(a["state_pool"][0]),
    }
    sent = {k: np.ascontiguousarray(v) for k, v in sent.items()}
    nc = bacc.Bacc("TRN2", target_bir_lowering=False, num_devices=1)
    t = {k: nc.dram_tensor(k, v.shape, F32, kind="ExternalInput").ap() for k, v in sent.items()}
    outs = {"y": [P, KT, TOK], "conv_p": [P, KT, CONV_BUF], "conv_s": [P, KT, CONV_BUF, NSAMP],
            "pool_p": [P, KT, POOL_BUF], "pool_s": [P, KT, POOL_BUF, NSAMP]}
    for k, shape in outs.items():
        t[k] = nc.dram_tensor(k, shape, F32, kind="ExternalOutput").ap()
    for k in ("y_conv", "sig_a", "sig_b", "silu_z"):
        t[k] = nc.dram_tensor(k, [P, KT, TOK], F32, kind="Internal").ap()
    build(nc, t)
    r = run_bass_kernel_spmd(nc, [sent], core_ids=[0]).results[0]

    def rows(x):
        return x.transpose(2, 1, 0).reshape(x.shape[2], D)

    y = rows(r["y"])
    samples = {k: r[k].transpose(3, 2, 1, 0).reshape(1, NSAMP, -1, D) for k in ("conv_s", "pool_s")}
    return (y[None, :SEQ], y[SEQ:, None], rows(r["conv_p"])[None, None], samples["conv_s"],
            rows(r["pool_p"])[None, None], samples["pool_s"])
```

```python
from contextlib import ExitStack

import concourse.bass as bass
from concourse import mybir

F32 = mybir.dt.float32
F32R = mybir.dt.float32r
ACT = mybir.ActivationFunctionType
ALU = mybir.AluOpType
AX_X = mybir.AxisListType.X

P = 128
D = 1024
SEQ = 1024
NSAMP = 8
TOK = SEQ + NSAMP
CHUNKS = 3
CW = TOK // CHUNKS
KT = D // P
PAIRS = KT // 2
CONV_W = 31
CONV_BUF = CONV_W - 1
POOL_MAX = 16
POOL_BUF = POOL_MAX - 1
DOUBLINGS = 4
NMOD = 1 + NSAMP
ADA_CHUNK = 512
ADA_BLOCKS = ADA_CHUNK // P
QUAD = 32
QUADS = P // QUAD
TOKBS = 4
TOKB = CW // TOKBS
RMS_EPS = 1e-6
LN_EPS = 1e-5

PAIR_JOBS = [
    ("glu_gate", 0, "act"), ("glu_value", 0, "dve"), ("glu_gate", 1, "act"), ("glu_value", 1, "dve"),
    ("merge_a", 0, "act"), ("merge_a", 1, "act"), ("merge_b", 0, "act"), ("merge_b", 1, "act"),
    ("pool_in", 0, "act"), ("pool_in", 1, "act"), ("pool_z", 0, "act"), ("pool_z", 1, "act"),
    ("pool_mix", 0, "dve"), ("conv_z", 0, "act"), ("pool_mix", 1, "dve"), ("conv_z", 1, "act"),
]
JOBS_PER_PAIR = len(PAIR_JOBS)
MAIN_PER_PAIR = sum(kind != "pool_mix" for kind, _, _ in PAIR_JOBS)
MIX_WIDTH = 2 * P
PAIR_TOTAL = PAIRS * JOBS_PER_PAIR
JOB_B = PAIR_TOTAL
JOB_A = JOB_B + KT
JOB_OUT = JOB_A + KT
JOBS = JOB_OUT + KT
W_IN_PART = {"glu_value": 0, "glu_gate": 1, "conv_z": 2, "pool_in": 3, "pool_z": 4, "merge_a": 5, "merge_b": 6}

TAPS_AT = {1: (1, 4), 2: (2, 5), 3: (0, 5), 4: (2, 5), 5: (2, 5), 6: (2, 5), 7: (2, 5), 8: (0, 1), 9: (0, 1), 10: (0, 4),
           12: (0, 6), 14: (0, 5)}
LAST_TAPS_AT = {1: (1, 5), 2: (2, 5), 3: (0, 5), 4: (2, 5), 5: (2, 5), 6: (2, 5), 7: (2, 6), 8: (0, 1), 9: (0, 1), 10: (0, 3),
                11: (0, 2), 12: (0, 6), 13: (0, 2)}
assert sum(map(sum, TAPS_AT.values())) == sum(map(sum, LAST_TAPS_AT.values())) == 2 * CONV_W

SHORT_NEXT = [i for i in range(JOBS_PER_PAIR - 1) if PAIR_JOBS[i + 1][0] == "pool_mix"]

WARM_SUMS = 10
WARM_ADA = ((0, 4), (0, 8), (0, 0), (0, 0))
WARM_TURN = (3, 9, 0, 0)
WARM_JOBS = 4
WARM_FINAL = 6
SUMS_0_AT = 5
SUMS_1_AT = 6
SPREAD_AT = 3

OUT_PARTS = [(0, 0, 4), (0, 4, KT), (1, 0, 4), (1, 4, KT), (2, 0, 2), (2, 2, 4), (2, 4, 6), (2, 6, KT)]

N_PAR = CONV_W + 2
N_POOLC = DOUBLINGS + 1 + 2 * POOL_MAX


def main_index(i):
    return sum(kind != "pool_mix" for kind, _, _ in PAIR_JOBS[:i])


def evacs(engine, i):
    return sum(e == engine for _, _, e in PAIR_JOBS[:i + 1])


ACT_EVACS = evacs("act", JOBS_PER_PAIR - 1)
DVE_EVACS = evacs("dve", JOBS_PER_PAIR - 1)


def build(nc, t):
    with ExitStack() as ctx:
        base = (nc.sbuf_base + 31) // 32 * 32

        def at(name, shape, dt, offset):
            return nc.alloc_sbuf_tensor_at(name, [P] + shape, dt, offset=offset)

        ROW = TOK * 4
        zone_h = base
        zone_g = zone_h + 2 * KT * ROW
        zone_b = zone_g + 2 * KT * ROW
        zone_rest = zone_b + KT * ROW
        hr = at("hr", [2 * KT, TOK], F32R, zone_h)
        hf = at("hf", [2 * KT, TOK], F32, zone_h)
        gr = at("gr", [2 * KT, TOK], F32R, zone_g)
        gf = at("gf", [2 * KT, TOK], F32, zone_g)
        bf = at("bf", [KT, TOK], F32, zone_b)
        br = at("br", [KT, TOK], F32R, zone_b)
        ada_raw = at("ada_raw", [4, KT, ADA_CHUNK], F32, zone_g)
        cursor = [zone_g]

        def g_place(name, shape, dt):
            size = 4
            for n in shape:
                size *= n
            o = cursor[0]
            cursor[0] += (size + 31) // 32 * 32
            return at(name, shape, dt, o)

        stage_lo = g_place("stage_lo", [2, TOK], F32)
        conv_y = g_place("conv_y", [2, TOK], F32)
        conv_u = g_place("conv_u", [2, CONV_BUF + TOK], F32)
        sig = g_place("sig", [TOK], F32)
        pool_u = g_place("pool_u", [2, POOL_MAX + TOK], F32)
        pool_s = g_place("pool_s", [2, POOL_MAX + SEQ], F32)
        pool_p = g_place("pool_p", [4, TOK], F32R)
        assert cursor[0] <= zone_b
        cursor[0] = zone_rest
        w_raw = g_place("w_raw", [2, KT * P], F32)
        w_hi = g_place("w_hi", [2, KT * P], F32R)
        w_lo = g_place("w_lo", [2, KT * P], F32R)
        row_mean = g_place("row_mean", [TOK], F32)
        stage_hi = g_place("stage_hi", [2, TOK], F32)
        ext_at = cursor[0]
        ext_conv = g_place("ext_conv", [2, CONV_W, NSAMP], F32)
        ext_pool = g_place("ext_pool", [2, POOL_MAX, NSAMP], F32)
        prod = g_place("prod", [CONV_W, NSAMP], F32)
        par_all = g_place("par_all", [PAIRS, 2, N_PAR], F32)
        poolc_all = g_place("poolc_all", [PAIRS, N_POOLC], F32)
        par = g_place("par", [2, N_PAR], F32)
        poolc = g_place("poolc", [N_POOLC], F32)
        vecs = g_place("vecs", [4, KT], F32)
        ada_b = g_place("ada_b", [6, ADA_BLOCKS], F32)
        c_in = g_place("c_in", [KT, NMOD], F32)
        c_act = g_place("c_act", [KT, QUAD], F32)
        pick = g_place("pick", [NMOD], F32)
        eye = g_place("eye", [TOKB], F32)
        tok_rstd = g_place("tok_rstd", [CHUNKS * TOKBS], F32)
        mod = g_place("mod", [6, ADA_BLOCKS, NMOD], F32)
        ones = g_place("ones", [P], F32)
        eps = g_place("eps", [2], F32)
        assert cursor[0] <= nc.sbuf_usable_end, cursor[0]
        ada_rows = at("ada_rows", [2, ADA_CHUNK], F32, zone_h + (2 * KT - 2) * ROW)
        gate_raw = at("gate_raw", [KT, ADA_CHUNK], F32, zone_g + 4 * ROW)
        gate_rows = at("gate_rows", [ADA_CHUNK], F32, ext_at)

        stage = [stage_lo[:, 0, :], stage_lo[:, 1, :], stage_hi[:, 0, :], stage_hi[:, 1, :]]
        sq_sum = stage_hi[:, 0, :]
        row_rstd = stage_hi[:, 1, :]
        full_a = stage_hi[:, 1, :]
        G_NORM, LN_G, LN_B, G_FINAL = range(4)

        ps = ctx.enter_context(nc.psum_tensor("ps", [P, 2, CHUNKS, 512], F32))
        aux = ctx.enter_context(nc.psum_tensor("aux", [P, 2, 512], F32))

        def ps_job(s):
            return ps[:, s % 2, :, 0:CW]

        ada_bank = [ps[:, 1, 0, :], ps[:, 1, 2, :], aux[:, 1, :], aux[:, 0, :]]

        def by_chunk(ap):
            return ap.rearrange("p (c t) -> p c t", c=CHUNKS)

        def cols(c):
            return slice(c * CW, (c + 1) * CW)

        def sem(name):
            return ctx.enter_context(nc.semaphore(name))

        c_loaded = sem("c_loaded")
        small_loaded = sem("small_loaded")
        par_loaded = sem("par_loaded")
        x_loaded = [sem(f"x_loaded{i}") for i in range(4)]
        ada_loaded = [[sem(f"ada_loaded{i}_{half}") for half in range(2)] for i in range(4)]
        gate_loaded = sem("gate_loaded")
        raw_full = [sem("raw_full0"), sem("raw_full1")]
        ext_loaded = sem("ext_loaded")
        sigb_loaded = [sem(f"sigb_loaded{i}") for i in range(4)]
        y_loaded = [sem(f"y_loaded{i}") for i in range(4)]
        siluz_loaded = sem("siluz_loaded")
        siga_loaded = [sem("siga_loaded0"), sem("siga_loaded1")]
        xres_loaded = [sem("xres_loaded0"), sem("xres_loaded1")]
        stage_free = [sem(f"stage_free{i}") for i in range(4)]
        y_free = [sem("y_free0"), sem("y_free1")]
        conv_state_stored = sem("conv_state_stored")
        pool_state_stored = sem("pool_state_stored")
        out_stored = sem("out_stored")
        c_padded = sem("c_padded")
        c_ready = sem("c_ready")
        ones_ready = sem("ones_ready")
        pads_ready = sem("pads_ready")
        ada_done = sem("ada_done")
        ada_rows_ready = sem("ada_rows_ready")
        ada_turned = sem("ada_turned")
        ada_mod_done = sem("ada_mod_done")
        x_squared = sem("x_squared")
        x_summed = sem("x_summed")
        x_var_done = sem("x_var_done")
        x_std_ready = sem("x_std_ready")
        h_scaled = sem("h_scaled")
        h_shifted = sem("h_shifted")
        h_hi_done = sem("h_hi_done")
        h_lo_done = sem("h_lo_done")
        gate_done = sem("gate_done")
        gate_rows_ready = sem("gate_rows_ready")
        gate_turned = sem("gate_turned")
        gate_ready = sem("gate_ready")
        w_hi_done = sem("w_hi_done")
        w_lo_done = sem("w_lo_done")
        pe_done = sem("pe_done")
        act_evac = sem("act_evac")
        dve_evac = sem("dve_evac")
        u_ready = sem("u_ready")
        conv_done = sem("conv_done")
        p_ready = sem("p_ready")
        p_hi_done = sem("p_hi_done")
        p_lo_done = sem("p_lo_done")
        y_summed = sem("y_summed")
        b_hi_done = sem("b_hi_done")
        b_lo_done = sem("b_lo_done")
        mean_done = sem("mean_done")
        mean_ready = sem("mean_ready")
        y_centred = sem("y_centred")
        y_squared = sem("y_squared")
        y_sq_summed = sem("y_sq_summed")
        y_var_done = sem("y_var_done")
        y_std_ready = sem("y_std_ready")
        y_normed = sem("y_normed")
        y_silu = sem("y_silu")
        a_full = sem("a_full")
        a_hi_done = sem("a_hi_done")
        a_lo_done = sem("a_lo_done")
        m_full = sem("m_full")
        m_hi_done = sem("m_hi_done")
        m_lo_done = sem("m_lo_done")
        x_new_ready = sem("x_new_ready")
        x_new_squared = sem("x_new_squared")
        x_new_summed = sem("x_new_summed")
        f_var_done = sem("f_var_done")
        f_std_ready = sem("f_std_ready")
        f_inverse_ready = sem("f_inverse_ready")
        f_spread = sem("f_spread")
        x_new_scaled = sem("x_new_scaled")
        y_out_ready = sem("y_out_ready")
        dve_chain = sem("dve_chain")

        LINKS = 1 + 2 * (1 + (2 + CONV_W) + (DOUBLINGS + 2 + 1))

        block = ctx.enter_context(nc.Block())

        @block.sync
        def _(sp):
            for n in range(4):
                sp.dma_start(bf[:, 2 * n:2 * n + 2, :], t["x_t"][:, 2 * n:2 * n + 2, :]).then_inc(x_loaded[n], 16)
            for s in range(2):
                sp.dma_start(w_raw[:, s, :], t["w_main"][s]).then_inc(raw_full[s], 16)
            for q in range(4):
                if q == 1:
                    sp.dma_start(pick[:], t["pick"]).then_inc(small_loaded, 16)
                    sp.dma_start(ada_b[:], t["ada_b"]).then_inc(small_loaded, 16)
                    sp.dma_start(vecs[:], t["vecs"]).then_inc(small_loaded, 16)
                    sp.dma_start(eye[:], t["eye"]).then_inc(small_loaded, 16)
                for half in range(2):
                    k = slice(half * KT // 2, (half + 1) * KT // 2)
                    sp.dma_start(ada_raw[:, q, k, :], t["w_ada"][q][:, k, :]).then_inc(ada_loaded[q][half], 16)
            sp.dma_start(par_all[:], t["par"]).then_inc(par_loaded, 16)
            sp.dma_start(poolc_all[:], t["poolc"]).then_inc(par_loaded, 16)

            with sp.Fori(0, PAIRS) as g:
                sp.wait_ge(conv_state_stored, g * 32 + 32)
                sp.wait_ge(pool_state_stored, g * 32 + 32)
                for i in range(JOBS_PER_PAIR):
                    sp.wait_ge(w_lo_done, g * JOBS_PER_PAIR + (i + 1))
                    n = (i + 2) % JOBS_PER_PAIR
                    if PAIR_JOBS[n][0] == "pool_mix":
                        sp.dma_start(w_raw[:, i % 2, 0:MIX_WIDTH],
                                     t["w_mix"][bass.ds(g * 2 + PAIR_JOBS[n][1], 1)].rearrange("a p n -> (a p) n")
                                     ).then_inc(raw_full[i % 2], 16)
                    else:
                        k = main_index(n) + (MAIN_PER_PAIR if i + 2 >= JOBS_PER_PAIR else 0)
                        sp.dma_start(w_raw[:, i % 2, :],
                                     t["w_main"][bass.ds(g * MAIN_PER_PAIR + k, 1)].rearrange("a p n -> (a p) n")
                                     ).then_inc(raw_full[i % 2], 16)
                    if i == 0:
                        sp.dma_start(ext_conv[:, :, 0:CONV_BUF, :], t["state_conv"][:, bass.ds(g * 2, 2)]).then_inc(ext_loaded, 16)
                        sp.dma_start(ext_pool[:, :, 0:POOL_BUF, :], t["state_pool"][:, bass.ds(g * 2, 2)]).then_inc(ext_loaded, 16)
                    if i == 8:
                        sp.wait_ge(u_ready, g * 4 + 2)
                        sp.dma_start(t["conv_p"][:, bass.ds(g * 2, 2)], conv_u[:, :, SEQ:SEQ + CONV_BUF]).then_inc(conv_state_stored, 16)
                        sp.dma_start(t["conv_s"][:, bass.ds(g * 2, 2)], ext_conv[:, :, 1:CONV_W, :]).then_inc(conv_state_stored, 16)
                    if i == 12:
                        sp.wait_ge(conv_done, g * 2 + 1)
                        sp.dma_start(t["y_conv"][:, bass.ds(g * 2, 1)], conv_y[:, 0:1, :]).then_inc(y_free[0], 16)
                        sp.wait_ge(u_ready, g * 4 + 4)
                        sp.dma_start(t["pool_p"][:, bass.ds(g * 2, 2)], pool_u[:, :, 1 + SEQ:POOL_MAX + SEQ]).then_inc(pool_state_stored, 16)
                        sp.dma_start(t["pool_s"][:, bass.ds(g * 2, 2)], ext_pool[:, :, 1:POOL_MAX, :]).then_inc(pool_state_stored, 16)
                sp.wait_ge(conv_done, g * 2 + 2)
                sp.dma_start(t["y_conv"][:, bass.ds(g * 2 + 1, 1)], conv_y[:, 1:2, :]).then_inc(y_free[1], 16)

            def load_main(s):
                sp.wait_ge(w_lo_done, s - 1)
                sp.dma_start(w_raw[:, s % 2, :], t["w_main"][s - PAIR_TOTAL + PAIRS * MAIN_PER_PAIR]).then_inc(raw_full[s % 2], 16)

            load_main(JOB_B + 2)
            for n in range(4):
                sp.wait_ge(b_lo_done, 2 * n + 2)
                if n == 0:
                    for x in range(2):
                        sp.wait_ge(y_free[x], 16 * (PAIRS + 1))
                sp.dma_start(bf[:, 2 * n:2 * n + 2, :], t["y_conv"][:, 2 * n:2 * n + 2]).then_inc(y_loaded[n], 16)
            load_main(JOB_B + 3)
            sp.wait_ge(pe_done, PAIR_TOTAL)
            for k in range(4):
                sp.wait_ge(stage_free[k], 16 * (PAIRS if k < 2 else 2 * PAIRS + 1))
            for n in range(4):
                rows = slice(2 * n, 2 * n + 2)
                sp.dma_start(hf[:, KT + 2 * n:KT + 2 * n + 2, :], t["sig_b"][:, rows]).then_inc(sigb_loaded[n], 16)
            load_main(JOB_B + 4)
            load_main(JOB_B + 5)
            sp.wait_ge(y_sq_summed, KT - 1)
            sp.dma_start(hf[:, 0:KT, :], t["silu_z"]).then_inc(siluz_loaded, 16)
            for s in range(JOB_B + 6, JOB_A + 2):
                load_main(s)
            sp.wait_ge(pe_done, JOB_A)
            sp.dma_start(gf[:, KT:KT + 2, :], t["sig_a"][:, 0:2]).then_inc(siga_loaded[0], 16)
            sp.dma_start(gate_raw[:], t["w_ada"][4]).then_inc(gate_loaded, 16)
            load_main(JOB_A + 2)
            sp.dma_start(gf[:, KT + 2:2 * KT, :], t["sig_a"][:, 2:KT]).then_inc(siga_loaded[1], 16)
            load_main(JOB_A + 3)
            load_main(JOB_A + 4)
            sp.wait_ge(gate_done, 1)
            sp.dma_start(gate_raw[:], t["w_ada"][5]).then_inc(gate_loaded, 16)
            for s in range(JOB_A + 5, JOB_OUT + 3):
                load_main(s)
            sp.wait_ge(pe_done, JOB_OUT)
            sp.dma_start(hf[:, 0:2, :], t["x_t"][:, 0:2]).then_inc(xres_loaded[0], 16)
            load_main(JOB_OUT + 3)
            sp.dma_start(hf[:, 2:KT, :], t["x_t"][:, 2:KT]).then_inc(xres_loaded[1], 16)
            for s in range(JOB_OUT + 4, JOBS):
                load_main(s)
            for n, (c, m0, m1) in enumerate(OUT_PARTS):
                sp.wait_ge(y_out_ready, n + 1)
                sp.dma_start(t["y"][:, m0:m1, cols(c)], hf[:, KT + m0:KT + m1, cols(c)]).then_inc(out_stored, 16)
            sp.wait_ge(out_stored, 16 * len(OUT_PARTS))
            sp.wait_ge(conv_state_stored, 32 * (PAIRS + 1))
            sp.wait_ge(pool_state_stored, 32 * (PAIRS + 1))

        @block.gpsimd
        def _(pool):
            nc.gpsimd.memset(c_act[:], 0.0).then_inc(c_padded, 1)
            nc.gpsimd.memset(ones[:], 1.0 / D)
            nc.gpsimd.memset(eps[:, 0:1], RMS_EPS)
            nc.gpsimd.memset(row_mean[:], 0.0)
            nc.gpsimd.memset(eps[:, 1:2], LN_EPS).then_inc(ones_ready, 1)
            pool.wait_ge(ada_done, 4)
            nc.gpsimd.memset(conv_u[:, :, 0:CONV_BUF], 0.0)
            nc.gpsimd.memset(pool_u[:, :, 0:POOL_MAX], 0.0)
            nc.gpsimd.memset(pool_s[:, :, 0:POOL_MAX], 0.0).then_inc(pads_ready, 1)

        @block.tensor
        def _(pe):
            def modulation_product(bank, k, w):
                quad = slice(k % QUADS * QUAD, (k % QUADS + 1) * QUAD)
                return nc.tensor.matmul(bank[quad, :], c_act[:, k, :], w[:, k, :], start=(k < QUADS), stop=(k >= KT - QUADS),
                                        tile_position=(0, k % QUADS * QUAD))

            def modulation_turn(bank, rows):
                for j in range(ADA_BLOCKS):
                    last = nc.tensor.matmul(bank[:, j * NMOD:(j + 1) * NMOD], rows[:, j * P:(j + 1) * P], pick[:], start=True, stop=True)
                return last

            def keep_warm(n):
                for _ in range(n):
                    nc.tensor.matmul(ps[:, 0, 0, 0:P], ones[:], ones[:], start=True, stop=True)

            def ada(q, half):
                if (q, half) == (0, 0):
                    pe.wait_ge(c_ready, 1)
                if q >= 2 and half == 0:
                    pe.wait_ge(x_std_ready, 4 - q)
                keep_warm(WARM_ADA[q][half])
                pe.wait_ge(ada_loaded[q][half], 16)
                for k in range(half * KT // 2, (half + 1) * KT // 2):
                    last = modulation_product(ada_bank[q], k, ada_raw[:, q, :, :])
                if half == 1:
                    last.then_inc(ada_done, 1)

            def turn(q):
                keep_warm(WARM_TURN[q])
                pe.wait_ge(ada_rows_ready, q + 1)
                modulation_turn(ada_bank[q], ada_rows[:, q % 2, :]).then_inc(ada_turned, 1)

            def token_sums(out, row, done):
                nc.tensor.matmul(out, ones[:], row, start=True, stop=True).then_inc(done, 1)

            pe.wait_ge(ones_ready, 1)
            pe.wait_ge(x_squared, KT - 2)
            keep_warm(WARM_SUMS)
            pe.wait_ge(x_summed, 1)
            token_sums(aux[:, 0, 0:CW], sq_sum[:, cols(0)], x_var_done)
            token_sums(aux[:, 1, 0:CW], sq_sum[:, cols(1)], x_var_done)
            token_sums(ps[:, 1, 1, 0:CW], sq_sum[:, cols(2)], x_var_done)
            def k_step(s_par, k, w_cols, rhs_hi, rhs_lo, n_k, chunks=range(CHUNKS)):
                wh = w_hi[:, s_par, w_cols]
                wl = w_lo[:, s_par, w_cols]
                for c in chunks:
                    out = ps[:, s_par, c, 0:CW]
                    nc.tensor.matmul(out, wh, rhs_hi[:, cols(c)], start=(k == 0), stop=False)
                    nc.tensor.matmul(out, wh, rhs_lo[:, cols(c)], start=False, stop=False)
                for c in chunks:
                    last = nc.tensor.matmul(ps[:, s_par, c, 0:CW], wl, rhs_hi[:, cols(c)], start=False, stop=(k == n_k - 1))
                return last

            def h_step(i, k):
                return k_step(i % 2, k, slice(k * P, (k + 1) * P), hr[:, k, :], hr[:, KT + k, :], KT)

            def pair_job(g, i):
                kind, tile, _ = PAIR_JOBS[i]
                pe.wait_ge(w_lo_done, g * JOBS_PER_PAIR + (i + 1))
                if i < 2:
                    pe.wait_ge(act_evac, g * ACT_EVACS + (i + 1))
                elif PAIR_JOBS[i - 2][2] == "act":
                    pe.wait_ge(act_evac, g * ACT_EVACS + (2 + evacs("act", i - 2)))
                else:
                    pe.wait_ge(dve_evac, g * DVE_EVACS + evacs("dve", i - 2))
                if kind == "pool_mix":
                    if tile == 0:
                        pe.wait_ge(p_lo_done, g * 2 + 2)
                    for k in range(2):
                        last = k_step(i % 2, k, slice(k * P, (k + 1) * P), pool_p[:, k, :], pool_p[:, 2 + k, :], 2)
                else:
                    for k in range(KT):
                        last = h_step(i, k)
                last.then_inc(pe_done, 1)

            together = KT - 3

            def side_by_side(k):
                if k == 0:
                    pe.wait_ge(w_lo_done, 2)
                    pe.wait_ge(ada_mod_done, 2)
                    pe.wait_ge(x_std_ready, CHUNKS)
                pe.wait_ge(h_lo_done, k + 1)
                h_step(0, k)
                h_step(1, k)

            for q in range(4):
                ada(q, 0)
                ada(q, 1)
                if q == 0:
                    pe.wait_ge(small_loaded, 64)
                if q >= 2:
                    pe.wait_ge(h_lo_done, q)
                    h_step(0, q - 1)
                if q == 3:
                    h_step(1, q - 1)
                turn(q)
                if q == 2:
                    h_step(1, q - 1)
                if q == 1:
                    keep_warm(WARM_JOBS)
                    side_by_side(0)
            for k in range(3, together):
                side_by_side(k)
            for i in range(2):
                for k in range(together, KT):
                    if i == 0:
                        pe.wait_ge(h_lo_done, k + 1)
                    last = h_step(i, k)
                last.then_inc(pe_done, 1)
            for i in range(2, JOBS_PER_PAIR):
                pair_job(0, i)
            with pe.Fori(1, PAIRS) as g:
                for i in range(JOBS_PER_PAIR):
                    pair_job(g, i)

            def job(s_par, hi, lo, after_k=None, before_k=None):
                for k in range(KT):
                    if before_k:
                        before_k(k)
                    last = k_step(s_par, k, slice(k * P, (k + 1) * P), hi[k], lo[k], KT)
                    if after_k:
                        after_k(k)
                last.then_inc(pe_done, 1)

            b_hi = [gr[:, k, :] for k in range(KT)]
            b_lo = [gr[:, KT + k, :] for k in range(KT)]

            def mean_third(k):
                if k == 3:
                    pe.wait_ge(mean_ready, 1)
                    token_sums(aux[:, 0, 0:CW], row_mean[:, cols(2)], mean_done)

            def var_sums(k):
                if k == 2:
                    pe.wait_ge(y_sq_summed, KT - 1)
                    pe.wait_ge(mean_ready, CHUNKS)
                    for c in range(2):
                        token_sums(aux[:, c, 0:CW], sq_sum[:, cols(c)], y_var_done)
                if k == 4:
                    pe.wait_ge(y_std_ready, 1)
                    token_sums(aux[:, 0, 0:CW], sq_sum[:, cols(2)], y_var_done)

            def job_pairs(first, count, hi, lo):
                with pe.Fori(0, count // 2) as r:
                    for odd in range(2):
                        pe.wait_ge(w_lo_done, r * 2 + (first + odd + 1))
                        pe.wait_ge(dve_evac, r * 2 + (PAIRS * DVE_EVACS + first + odd - 1 - JOB_B))
                        job((first + odd) % 2, hi, lo)

            pe.wait_ge(y_summed, 2 * PAIRS)
            for c in range(2):
                token_sums(aux[:, c, 0:CW], row_mean[:, cols(c)], mean_done)
            for s in range(JOB_B, JOB_B + 4):
                pe.wait_ge(w_lo_done, s + 1)
                if s == JOB_B:
                    pe.wait_ge(dve_evac, PAIRS * DVE_EVACS)
                elif s == JOB_B + 1:
                    pe.wait_ge(act_evac, 2 + PAIRS * ACT_EVACS)
                else:
                    pe.wait_ge(dve_evac, PAIRS * DVE_EVACS + s - 1 - JOB_B)
                job(s % 2, b_hi, b_lo,
                    after_k={JOB_B: mean_third, JOB_B + 3: var_sums}.get(s),
                    before_k=(lambda k: pe.wait_ge(b_lo_done, k + 1)) if s == JOB_B else None)

            job_pairs(JOB_B + 4, 4, b_hi, b_lo)
            a_hi = [br[:, k, :] for k in range(KT)]
            a_lo = [hr[:, k, :] for k in range(KT)]

            def single(s, hi, lo, before_k=None):
                pe.wait_ge(w_lo_done, s + 1)
                pe.wait_ge(dve_evac, PAIRS * DVE_EVACS + s - 1 - JOB_B)
                job(s % 2, hi, lo, before_k=before_k)

            def gate_chunk(n):
                pe.wait_ge(gate_loaded, 16 * (n + 1))
                for k in range(KT):
                    last = modulation_product(aux[:, n, :], k, gate_raw)
                last.then_inc(gate_done, 1)

            def gate_turn(n):
                pe.wait_ge(gate_rows_ready, n + 1)
                modulation_turn(aux[:, n, :], gate_rows).then_inc(gate_turned, 1)

            single(JOB_A, a_hi, a_lo, before_k=lambda k: pe.wait_ge(a_lo_done, k + 1))
            job_pairs(JOB_A + 1, 2, a_hi, a_lo)
            gate_chunk(0)
            single(JOB_A + 3, a_hi, a_lo)
            gate_turn(0)
            gate_chunk(1)
            single(JOB_A + 4, a_hi, a_lo)
            gate_turn(1)
            single(JOB_A + 5, a_hi, a_lo)
            job_pairs(JOB_A + 6, 2, a_hi, a_lo)
            m_hi, m_lo = b_hi, b_lo
            single(JOB_OUT, m_hi, m_lo, before_k=lambda k: pe.wait_ge(m_lo_done, k + 1))
            job_pairs(JOB_OUT + 1, 4, m_hi, m_lo)
            single(JOB_OUT + 5, m_hi, m_lo)

            def token_columns(c, rows):
                for b in range(TOKBS):
                    for n, row in enumerate(rows):
                        t0 = c * CW + b * TOKB
                        last = nc.tensor.matmul(aux[0:TOKB, c % 2, b:b + 1], row[:, t0:t0 + TOKB], ones[:, 0:1],
                                                start=(n == 0), stop=(n == len(rows) - 1))
                last.then_inc(f_var_done, 1)

            def spread(c):
                pe.wait_ge(f_inverse_ready, c)
                for b in range(TOKBS):
                    column = tok_rstd[0:TOKB, c * TOKBS + b:c * TOKBS + b + 1]
                    last = nc.tensor.matmul(aux[:, c % 2, b * TOKB:(b + 1) * TOKB], column.broadcast_to([TOKB, P]),
                                            eye[0:TOKB, :], start=True, stop=True)
                last.then_inc(f_spread, 1)

            def last_product(c, s, after_k={}):
                if c == 0:
                    pe.wait_ge(w_lo_done, s + 1)
                    pe.wait_ge(dve_evac, PAIRS * DVE_EVACS + s - 1 - JOB_B)
                for k in range(KT):
                    last = k_step(s % 2, k, slice(k * P, (k + 1) * P), m_hi[k], m_lo[k], KT, chunks=[c])
                    if k in after_k:
                        after_k[k]()
                last.then_inc(pe_done, 1)

            def sums_0():
                pe.wait_ge(x_new_summed, 1)
                token_sums(aux[:, 0, 0:CW], sq_sum[:, cols(0)], f_var_done)

            def sums_1():
                pe.wait_ge(x_new_summed, 2)
                token_columns(1, [sq_sum])

            last_product(0, JOBS - 2)
            last_product(0, JOBS - 1)
            last_product(1, JOBS - 2, {SUMS_0_AT: sums_0})
            last_product(1, JOBS - 1)
            last_product(2, JOBS - 2, {SUMS_1_AT: sums_1})
            last_product(2, JOBS - 1, {SPREAD_AT: lambda: spread(1)})
            pe.wait_ge(x_new_ready, KT)
            keep_warm(WARM_FINAL)
            pe.wait_ge(f_std_ready, 1)
            pe.wait_ge(x_new_summed, 3)
            pe.wait_ge(x_new_squared, KT - 2 + 2 * CHUNKS)
            token_columns(2, [sq_sum, bf[:, KT - 1, :]])
            spread(2)

        def weight_columns(i):
            return MIX_WIDTH if PAIR_JOBS[i % JOBS_PER_PAIR][0] == "pool_mix" else KT * P

        @block.scalar
        def _(act):
            def split_hi(slot, n, loaded):
                act.wait_ge(raw_full[slot], loaded)
                nc.scalar.activation(w_hi[:, slot, 0:n], w_raw[:, slot, 0:n], ACT.Copy).then_inc(w_hi_done, 1)

            act.dma_start(c_in[:], t["c_t"]).then_inc(c_loaded, 16)

            act.sem_inc(act_evac, 2)
            act.sem_inc(stage_free[2], 16)
            act.sem_inc(stage_free[3], 16)
            act.sem_inc(y_free[0], 16)
            act.sem_inc(y_free[1], 16)
            act.sem_inc(conv_state_stored, 32)
            act.sem_inc(pool_state_stored, 32)

            act.wait_ge(c_loaded, 16)
            act.wait_ge(c_padded, 1)
            nc.scalar.activation(c_act[:, :, 0:NMOD], c_in[:], ACT.Silu).then_inc(c_ready, 1)

            def ada_out(q):
                act.wait_ge(ada_done, q + 1)
                if q >= 2:
                    act.wait_ge(ada_turned, q - 1)
                nc.scalar.activation(ada_rows[:, q % 2, :], ada_bank[q], ACT.Copy).then_inc(ada_rows_ready, 1)

            def h_hi(e):
                act.wait_ge(h_scaled, e + 1)
                nc.scalar.activation(bf[:, e, 0:SEQ], bf[:, e, 0:SEQ], ACT.Identity, bias=mod[:, e // 2, e % 2, 0:1]).then_inc(h_shifted, 1)
                act.wait_ge(h_shifted, e + 1)
                nc.scalar.activation(hr[:, e, :], bf[:, e, :], ACT.Copy).then_inc(h_hi_done, 1)

            for e in range(KT):
                act.wait_ge(x_loaded[e // 2], 16)
                nc.scalar.activation(hf[:, e, :], bf[:, e, :], ACT.Square).then_inc(x_squared, 1)
            for s in range(2):
                split_hi(s, KT * P, 16)
            for c in range(CHUNKS):
                src = ps[:, 1, 1, 0:CW] if c == 2 else aux[:, c, 0:CW]
                act.wait_ge(x_var_done, c + 1)
                nc.scalar.activation(row_rstd[:, cols(c)], src, ACT.Sqrt, bias=eps[:, 0:1]).then_inc(x_std_ready, 1)
            ada_out(0)
            for e in range(KT):
                h_hi(e)
                if e % 2 == 0 and e // 2 + 1 < 4:
                    ada_out(e // 2 + 1)
            STAGED = {4: (0, "sig_a"), 5: (1, "sig_a"), 6: (2, "sig_b"), 7: (3, "sig_b"), 13: (2, "silu_z"), 15: (3, "silu_z")}

            def pair_step(g, i):
                kind, tile, engine = PAIR_JOBS[i]
                act.wait_ge(pe_done, g * JOBS_PER_PAIR + (i + 1))
                raw_count = g * (JOBS_PER_PAIR // 2 * 16) + 16 * ((i + 2) // 2 + 1)
                if i in SHORT_NEXT:
                    split_hi(i % 2, weight_columns(i + 2), raw_count)
                if engine == "act":
                    src = ps_job(i)
                    if kind == "glu_gate":
                        if tile == 1:
                            act.wait_ge(dve_evac, g * DVE_EVACS + 1)
                        dst, func = sig[:], ACT.Sigmoid
                    elif kind in ("merge_a", "merge_b"):
                        slot = STAGED[i][0]
                        if slot >= 2:
                            act.wait_ge(stage_free[slot], g * 32 + 16)
                        dst, func = stage[slot], ACT.Sigmoid
                    elif kind == "pool_in":
                        if tile == 0:
                            act.wait_ge(pool_state_stored, g * 32 + 32)
                        dst, func = pool_u[:, tile, POOL_MAX:POOL_MAX + TOK], ACT.Copy
                    elif kind == "pool_z":
                        act.wait_ge(stage_free[tile], g * 16 + 16)
                        dst, func = stage[tile], ACT.Silu
                    else:
                        act.wait_ge(stage_free[2 + tile], g * 32 + 32)
                        dst, func = stage[2 + tile], ACT.Silu
                    nc.scalar.activation(by_chunk(dst), src, func).then_inc(act_evac, 1)
                if i not in SHORT_NEXT:
                    split_hi(i % 2, weight_columns(i + 2), raw_count)
                if i in STAGED:
                    slot, name = STAGED[i]
                    act.wait_ge(act_evac, g * ACT_EVACS + (2 + evacs("act", i)))
                    act.dma_start(t[name][:, bass.ds(g * 2 + tile, 1)] if not isinstance(g, int) else t[name][:, 2 * g + tile:2 * g + tile + 1],
                                  stage[slot].rearrange("p (a t) -> p a t", a=1)).then_inc(stage_free[slot], 16)
                if i in (8, 9):
                    act.wait_ge(p_ready, g * 2 + (i - 7))
                    nc.scalar.activation(pool_p[:, tile, :], sig[:], ACT.Copy).then_inc(p_hi_done, 1)

            with act.Fori(0, PAIRS - 1) as g:
                for i in range(JOBS_PER_PAIR):
                    pair_step(g, i)
            for i in range(JOBS_PER_PAIR - 1):
                pair_step(PAIRS - 1, i)
            for e in range(KT):
                if e == 0:
                    act.wait_ge(dve_evac, PAIRS * DVE_EVACS)
                    act.wait_ge(y_free[0], 16 * (PAIRS + 1))
                    act.wait_ge(y_free[1], 16 * (PAIRS + 1))
                    act.wait_ge(conv_state_stored, 32 * (PAIRS + 1))
                    act.wait_ge(pool_state_stored, 32 * (PAIRS + 1))
                    act.wait_ge(p_lo_done, 2 * PAIRS)
                    act.wait_ge(y_summed, 2 * PAIRS)
                nc.scalar.activation(gr[:, e, :], bf[:, e, :], ACT.Copy).then_inc(b_hi_done, 1)
            pair_step(PAIRS - 1, JOBS_PER_PAIR - 1)

            def split_for(s):
                if s + 2 < JOBS:
                    act.wait_ge(pe_done, s + 1)
                    split_hi(s % 2, KT * P, 16 * ((s + 2) // 2 + 1))

            for c in range(CHUNKS):
                act.wait_ge(mean_done, c + 1)
                nc.scalar.activation(row_mean[:, cols(c)], aux[:, c % 2, 0:CW], ACT.Copy).then_inc(mean_ready, 1)
            for e in range(KT):
                if e == 4:
                    split_for(JOB_B)
                act.wait_ge(y_centred, e + 1)
                nc.scalar.activation(hf[:, e, :], bf[:, e, :], ACT.Square).then_inc(y_squared, 1)
            split_for(JOB_B + 1)
            split_for(JOB_B + 2)
            for c in range(CHUNKS):
                act.wait_ge(y_var_done, c + 1)
                nc.scalar.activation(row_rstd[:, cols(c)], aux[:, c % 2, 0:CW], ACT.Sqrt, bias=eps[:, 1:2]).then_inc(y_std_ready, 1)

            def silu_y(e):
                act.wait_ge(y_normed, e + 1)
                nc.scalar.activation(bf[:, e, :], bf[:, e, :], ACT.Silu, bias=vecs[:, LN_B, e:e + 1],
                                     scale=vecs[:, LN_G, e:e + 1]).then_inc(y_silu, 1)

            silu_y(0)
            silu_y(1)
            split_for(JOB_B + 3)
            for e in range(KT):
                act.wait_ge(a_full, e + 1)
                nc.scalar.activation(br[:, e, :], full_a, ACT.Copy).then_inc(a_hi_done, 1)
                if e in (1, 3, 5):
                    split_for(JOB_B + 4 + e // 2)
                if e + 2 < KT:
                    silu_y(e + 2)
            split_for(JOB_B + 7)
            for m in range(KT):
                if m in (3, 4):
                    n = m - 3
                    act.wait_ge(gate_done, n + 1)
                    nc.scalar.activation(gate_rows[:], aux[:, n, :], ACT.Copy).then_inc(gate_rows_ready, 1)
                split_for(JOB_A + m)
                act.wait_ge(m_full, m + 1)
                nc.scalar.activation(gr[:, m, :], hf[:, KT + m, :], ACT.Copy).then_inc(m_hi_done, 1)
            def final_square(n, m, t0, t1):
                row = hf[:, KT + m, t0:t1]
                act.wait_ge(x_new_ready, n + 1)
                nc.scalar.activation(bf[:, m, t0:t1], row, ACT.Square).then_inc(x_new_squared, 1)
                act.wait_ge(x_new_squared, n + 1)
                nc.scalar.activation(row, row, ACT.Copy, scale=vecs[:, G_FINAL, m:m + 1]).then_inc(x_new_scaled, 1)

            for m in range(KT - 2):
                split_for(JOB_OUT + m)
                final_square(m, m, 0, TOK)
            for c in range(CHUNKS):
                for j in range(2):
                    final_square(KT - 2 + 2 * c + j, KT - 2 + j, c * CW, (c + 1) * CW)
                act.wait_ge(f_var_done, c + 1)
                if c == 0:
                    nc.scalar.activation(row_rstd[:, cols(c)], aux[:, 0, 0:CW], ACT.Sqrt, bias=eps[:, 0:1]).then_inc(f_std_ready, 1)
                else:
                    nc.scalar.activation(tok_rstd[0:TOKB, c * TOKBS:(c + 1) * TOKBS], aux[0:TOKB, c % 2, 0:TOKBS], ACT.Sqrt,
                                         bias=eps[0:TOKB, 0:1]).then_inc(f_std_ready, 1)

        @block.vector
        def _(dve):
            v = nc.vector
            links = [0]
            at_pair = [None]

            def link(ins):
                links[0] += 1
                ins.then_inc(dve_chain, 1)
                g = at_pair[0]
                dve.wait_ge(dve_chain, links[0] if g is None else g * LINKS + links[0])

            def split_lo(slot, n, count):
                dve.wait_ge(w_hi_done, count)
                v.tensor_tensor(w_lo[:, slot, 0:n], w_raw[:, slot, 0:n], w_hi[:, slot, 0:n].bitcast(F32), ALU.subtract).then_inc(w_lo_done, 1)

            def wide(ap, n):
                return ap.unsqueeze(2).broadcast_to([P, ap.shape[1], n])

            for e in range(1, KT):
                dve.wait_ge(x_squared, e + 1)
                link(v.tensor_tensor(sq_sum, hf[:, 0, :] if e == 1 else sq_sum, hf[:, e, :], ALU.add))
            dve.sem_inc(x_summed, 1)

            def modulation(q):
                dve.wait_ge(ada_turned, q + 1)
                link(v.tensor_tensor(mod[:, q, :, :], ada_bank[q][:, 0:ADA_BLOCKS * NMOD].rearrange("p (j n) -> p j n", j=ADA_BLOCKS),
                                     wide(ada_b[:, q, :], NMOD), ALU.add))
                link(v.scalar_tensor_tensor(out=mod[:, q, 2:4, :], in0=mod[:, q, 2:4, :], scalar=1.0,
                                                in1=wide(vecs[:, G_NORM, 2 * q:2 * q + 2], NMOD), op0=ALU.add, op1=ALU.mult))
                dve.sem_inc(ada_mod_done, 1)

            split_lo(0, KT * P, 1)
            for c in range(CHUNKS):
                dve.wait_ge(x_std_ready, c + 1)
                link(v.reciprocal(row_rstd[:, cols(c)], row_rstd[:, cols(c)]))
            dve.wait_ge(small_loaded, 64)

            def h_samples(q):
                xs = bf[:, 2 * q:2 * q + 2, SEQ:TOK]
                link(v.tensor_tensor(xs, xs, mod[:, q, 2:4, 1:NMOD], ALU.mult))
                link(v.tensor_tensor(xs, xs, row_rstd[:, SEQ:TOK].unsqueeze(1).broadcast_to([P, 2, NSAMP]), ALU.mult))
                v.tensor_tensor(xs, xs, mod[:, q, 0:2, 1:NMOD], ALU.add)

            def h_tile(e):
                q, j = e // 2, e % 2
                xp = bf[:, e, 0:SEQ]
                v.scalar_tensor_tensor(out=xp, in0=xp, scalar=mod[:, q, 2 + j, 0:1], in1=row_rstd[:, 0:SEQ], op0=ALU.mult, op1=ALU.mult).then_inc(h_scaled, 1)

            def h_lo(e):
                dve.wait_ge(h_hi_done, e + 1)
                v.tensor_tensor(hr[:, KT + e, :], bf[:, e, :], hr[:, e, :].bitcast(F32), ALU.subtract).then_inc(h_lo_done, 1)

            for q in range(4):
                modulation(q)
                h_samples(q)
                h_tile(2 * q)
                if q >= 1:
                    h_lo(2 * q - 1)
                h_tile(2 * q + 1)
                if q == 0:
                    split_lo(1, KT * P, 2)
                h_lo(2 * q)
            h_lo(KT - 1)
            dve.wait_ge(pads_ready, 1)
            dve.wait_ge(par_loaded, 32)

            base_links = links[0]
            LEVELS = [pool_u, pool_s]

            def tap(x, k):
                y = conv_y[:, x, 0:SEQ]
                if k == 0:
                    return v.tensor_scalar(y, conv_u[:, x, 0:SEQ], par[:, x, 0:1], par[:, x, CONV_W:CONV_W + 1], ALU.mult, ALU.add)
                return v.scalar_tensor_tensor(out=y, in0=conv_u[:, x, k:k + SEQ], scalar=par[:, x, k:k + 1], in1=y, op0=ALU.mult, op1=ALU.add)

            def conv_samples(g, x):
                if x == 0:
                    dve.wait_ge(ext_loaded, g * 32 + 32)
                ys = conv_y[:, x, SEQ:TOK]
                link(v.tensor_tensor(prod[:], ext_conv[:, x, :, :], wide(par[:, x, 0:CONV_W], NSAMP), ALU.mult))
                link(v.tensor_reduce(ys, prod[:].rearrange("p k s -> p s k"), AX_X, ALU.add))
                v.tensor_scalar(ys, ys, par[:, x, CONV_W:CONV_W + 1], None, ALU.add)

            def taps(g, n):
                for _ in range(n):
                    x, k = divmod(tap_at[0], CONV_W)
                    if k == 0:
                        dve.wait_ge(y_free[x], g * 16 + 16)
                        conv_samples(g, x)
                    link(tap(x, k))
                    if k == CONV_W - 1:
                        v.tensor_tensor(row_mean[:], row_mean[:], conv_y[:, x, :], ALU.add).then_inc(y_summed, 1)
                        dve.sem_inc(conv_done, 1)
                    tap_at[0] += 1

            def pool_tile(g, x, split):
                u = pool_u[:, x, :]
                levels = [u, pool_s[:, 0, :], pool_s[:, 1, :], pool_s[:, 0, :], pool_s[:, 1, :]]
                for n in range(DOUBLINGS):
                    src, dst = levels[n], levels[n + 1]
                    back = 1 << n
                    link(v.scalar_tensor_tensor(out=dst[:, POOL_MAX:POOL_MAX + SEQ], in0=src[:, POOL_MAX - back:POOL_MAX + SEQ - back],
                                                scalar=poolc[:, n:n + 1], in1=src[:, POOL_MAX:POOL_MAX + SEQ], op0=ALU.mult, op1=ALU.add))
                    if n == 0:
                        split()
                full = sig[:]
                sums = levels[DOUBLINGS]
                v.scalar_tensor_tensor(out=full[:, POOL_MAX:SEQ], in0=sums[:, 2 * POOL_MAX:POOL_MAX + SEQ], scalar=poolc[:, DOUBLINGS:DOUBLINGS + 1],
                                       in1=u[:, 2 * POOL_MAX:POOL_MAX + SEQ], op0=ALU.mult, op1=ALU.subtract)
                inv = poolc[:, DOUBLINGS + 1:DOUBLINGS + 1 + POOL_MAX]
                v.tensor_tensor(full[:, 0:POOL_MAX], sums[:, POOL_MAX:2 * POOL_MAX], inv, ALU.mult)
                win = poolc[:, DOUBLINGS + 1 + POOL_MAX:N_POOLC]
                link(v.tensor_tensor(prod[:, 0:POOL_MAX, :], ext_pool[:, x, :, :], wide(win, NSAMP), ALU.mult))
                link(v.tensor_reduce(full[:, SEQ:TOK], prod[:, 0:POOL_MAX, :].rearrange("p k s -> p s k"), AX_X, ALU.add))
                v.tensor_tensor(full[:, 0:POOL_MAX], full[:, 0:POOL_MAX], u[:, POOL_MAX:2 * POOL_MAX], ALU.subtract)
                v.tensor_tensor(full[:, SEQ:TOK], full[:, SEQ:TOK], u[:, POOL_MAX + SEQ:POOL_MAX + TOK], ALU.subtract).then_inc(p_ready, 1)

            def pool_lo(g, x):
                dve.wait_ge(p_hi_done, g * 2 + (x + 1))
                link(v.tensor_tensor(pool_p[:, 2 + x, :], sig[:], pool_p[:, x, :].bitcast(F32), ALU.subtract))
                dve.sem_inc(p_lo_done, 1)

            tap_at = [0]

            def pair_step(g, i):
                kind, tile, engine = PAIR_JOBS[i]
                dve.wait_ge(pe_done, g * JOBS_PER_PAIR + (i + 1))
                if i == 0:
                    tap_at[0] = 0
                    if isinstance(g, int):
                        v.tensor_copy(par[:], par_all[:, g, :, :])
                        link(v.tensor_copy(poolc[:], poolc_all[:, g, :]))
                    else:
                        v.tensor_copy(par[:], par_all[:, bass.ds(g, 1), :, :].rearrange("p a x n -> p (a x) n"))
                        link(v.tensor_copy(poolc[:], poolc_all[:, bass.ds(g, 1), :].rearrange("p a n -> p (a n)")))
                if kind == "glu_value":
                    dve.wait_ge(act_evac, g * ACT_EVACS + (2 + evacs("act", i - 1)))
                    if tile == 0:
                        dve.wait_ge(conv_state_stored, g * 32 + 32)
                        dve.wait_ge(ext_loaded, g * 32 + 32)
                    link(v.tensor_tensor(by_chunk(conv_u[:, tile, CONV_BUF:CONV_BUF + TOK]), ps_job(i), by_chunk(sig[:]), ALU.mult))
                    dve.sem_inc(dve_evac, 1)
                    v.tensor_copy(ext_conv[:, tile, CONV_BUF, :], conv_u[:, tile, CONV_BUF + SEQ:CONV_BUF + TOK]).then_inc(u_ready, 1)
                    dve.wait_ge(u_ready, g * 4 + (tile + 1))
                if kind == "pool_mix":
                    dve.wait_ge(act_evac, g * ACT_EVACS + (2 + evacs("act", 10 + tile)))
                    e = g * 2 + tile
                    dst = bf[:, e, :] if isinstance(g, int) else bf[:, bass.ds(e, 1), :].rearrange("p a t -> p (a t)")
                    v.scalar_tensor_tensor(out=by_chunk(dst), in0=ps_job(i), scalar=par[:, tile, CONV_W + 1:CONV_W + 2],
                                           in1=by_chunk(stage[tile]), op0=ALU.mult, op1=ALU.mult).then_inc(dve_evac, 1)
                def split():
                    split_lo(i % 2, weight_columns(i + 2), g * JOBS_PER_PAIR + (i + 3))

                before, after = (LAST_TAPS_AT if isinstance(g, int) else TAPS_AT).get(i, (0, 0))
                taps(g, before)
                if i in (8, 9):
                    dve.wait_ge(act_evac, g * ACT_EVACS + (2 + evacs("act", i)))
                    if tile == 1:
                        pool_lo(g, 0)
                    v.tensor_copy(ext_pool[:, tile, POOL_BUF, :], pool_u[:, tile, POOL_MAX + SEQ:POOL_MAX + TOK]).then_inc(u_ready, 1)
                    pool_tile(g, tile, split)
                if i == 10:
                    pool_lo(g, 1)
                if i not in (8, 9):
                    split()
                taps(g, after)

            with dve.Fori(0, PAIRS - 1) as g:
                at_pair[0] = g
                for i in range(JOBS_PER_PAIR):
                    pair_step(g, i)
                assert links[0] - base_links == LINKS, (links[0] - base_links, LINKS)
            at_pair[0] = None
            links[0] = base_links + (PAIRS - 1) * LINKS
            for i in range(JOBS_PER_PAIR - 1):
                pair_step(PAIRS - 1, i)
            for e in range(KT):
                dve.wait_ge(b_hi_done, e + 1)
                v.tensor_tensor(gr[:, KT + e, :], bf[:, e, :], gr[:, e, :].bitcast(F32), ALU.subtract).then_inc(b_lo_done, 1)
            pair_step(PAIRS - 1, JOBS_PER_PAIR - 1)

            def split_for(s):
                if s + 2 < JOBS:
                    split_lo(s % 2, KT * P, s + 3)

            def merge_b(m):
                s = JOB_B + m
                dve.wait_ge(pe_done, s + 1)
                dve.wait_ge(sigb_loaded[m // 2], 16)
                row = hf[:, KT + m, :]
                v.tensor_tensor(by_chunk(row), ps_job(s), by_chunk(row), ALU.mult).then_inc(dve_evac, 1)

            dve.wait_ge(mean_ready, CHUNKS)
            for e in range(KT):
                dve.wait_ge(y_loaded[e // 2], 16)
                v.tensor_tensor(bf[:, e, :], bf[:, e, :], row_mean[:], ALU.subtract).then_inc(y_centred, 1)
                if e == 5:
                    merge_b(0)
                    split_for(JOB_B)
            for e in range(1, KT):
                dve.wait_ge(y_squared, e + 1)
                v.tensor_tensor(sq_sum, hf[:, 0, :] if e == 1 else sq_sum, hf[:, e, :], ALU.add).then_inc(y_sq_summed, 1)
                dve.wait_ge(y_sq_summed, e)
                if e == 4:
                    merge_b(1)
                    split_for(JOB_B + 1)
            merge_b(2)
            split_for(JOB_B + 2)
            for c in range(CHUNKS):
                dve.wait_ge(y_std_ready, c + 1)
                link(v.reciprocal(row_rstd[:, cols(c)], row_rstd[:, cols(c)]))
            for e in range(KT):
                if e == 3:
                    merge_b(3)
                    split_for(JOB_B + 3)
                last = v.tensor_tensor(bf[:, e, :], bf[:, e, :], row_rstd, ALU.mult)
                last.then_inc(y_normed, 1)
            dve.wait_ge(siluz_loaded, 16)
            dve.wait_ge(y_normed, KT)
            for e in range(KT):
                dve.wait_ge(y_silu, e + 1)
                v.tensor_tensor(full_a, bf[:, e, :], hf[:, e, :], ALU.mult).then_inc(a_full, 1)
                if e in (1, 3, 5):
                    merge_b(4 + e // 2)
                    split_for(JOB_B + 4 + e // 2)
                dve.wait_ge(a_hi_done, e + 1)
                link(v.tensor_tensor(hr[:, e, :], full_a, br[:, e, :].bitcast(F32), ALU.subtract))
                dve.sem_inc(a_lo_done, 1)
            merge_b(7)
            split_for(JOB_B + 7)

            for m in range(KT):
                s = JOB_A + m
                dve.wait_ge(pe_done, s + 1)
                dve.wait_ge(siga_loaded[min(m // 2, 1)], 16)
                t_row, m_row = gf[:, KT + m, :], hf[:, KT + m, :]
                v.tensor_tensor(by_chunk(t_row), ps_job(s), by_chunk(t_row), ALU.mult).then_inc(dve_evac, 1)
                dve.wait_ge(dve_evac, PAIRS * DVE_EVACS + s + 1 - JOB_B)
                v.tensor_tensor(m_row, t_row, m_row, ALU.add).then_inc(m_full, 1)
                split_for(s)
                dve.wait_ge(m_hi_done, m + 1)
                v.tensor_tensor(gr[:, KT + m, :], m_row, gr[:, m, :].bitcast(F32), ALU.subtract).then_inc(m_lo_done, 1)
                if m in (4, 5):
                    n = m - 4
                    dve.wait_ge(gate_turned, n + 1)
                    v.tensor_tensor(mod[:, 4 + n, :, :], aux[:, n, 0:ADA_BLOCKS * NMOD].rearrange("p (j n) -> p j n", j=ADA_BLOCKS),
                                    wide(ada_b[:, 4 + n, :], NMOD), ALU.add).then_inc(gate_ready, 1)

            def new_x(m, c0, c1):
                gate = mod[:, 4 + m // 4, m % 4, :]
                for c in range(c0, c1):
                    w = min(CW, SEQ - c * CW)
                    last = v.scalar_tensor_tensor(out=hf[:, KT + m, c * CW:c * CW + w], in0=ps[:, (JOB_OUT + m) % 2, c, 0:w],
                                                  scalar=gate[:, 0:1], in1=hf[:, m, c * CW:c * CW + w], op0=ALU.mult, op1=ALU.add)
                if c1 == CHUNKS:
                    xs = hf[:, KT + m, SEQ:TOK]
                    link(v.tensor_tensor(xs, ps[:, (JOB_OUT + m) % 2, CHUNKS - 1, CW - NSAMP:CW], gate[:, 1:NMOD], ALU.mult))
                    last = v.tensor_tensor(xs, xs, hf[:, m, SEQ:TOK], ALU.add)
                return last

            dve.wait_ge(gate_ready, 2)
            for m in range(KT - 2):
                dve.wait_ge(pe_done, JOB_OUT + m + 1)
                dve.wait_ge(xres_loaded[min(m // 2, 1)], 16)
                link(new_x(m, 0, CHUNKS))
                dve.sem_inc(dve_evac, 1)
                dve.sem_inc(x_new_ready, 1)
                split_for(JOB_OUT + m)
                if m >= 1:
                    dve.wait_ge(x_new_squared, m + 1)
                    link(v.tensor_tensor(sq_sum, bf[:, 0, :] if m == 1 else sq_sum, bf[:, m, :], ALU.add))

            def last_x(c, m):
                n = 2 * c + m - (KT - 2)
                dve.wait_ge(pe_done, JOBS - 2 + n + 1)
                new_x(m, c, c + 1).then_inc(x_new_ready, 1)

            def last_sum(c, tiles):
                for m in tiles:
                    dve.wait_ge(x_new_squared, 2 * c + m + 1)
                    ins = v.tensor_tensor(sq_sum[:, cols(c)], sq_sum[:, cols(c)], bf[:, m, cols(c)], ALU.add)
                    if m != tiles[-1]:
                        link(ins)
                ins.then_inc(x_new_summed, 1)

            def inverse(c):
                dve.wait_ge(f_std_ready, c + 1)
                column = tok_rstd[0:TOKB, c * TOKBS:(c + 1) * TOKBS]
                v.reciprocal(column, column).then_inc(f_inverse_ready, 1)

            parts = iter(OUT_PARTS)

            def norm(rstd):
                c, m0, m1 = next(parts)
                dve.wait_ge(x_new_scaled, KT + 2 * c)
                rows = hf[:, KT + m0:KT + m1, cols(c)]
                v.tensor_tensor(rows, rows, rstd.unsqueeze(1).broadcast_to([P, m1 - m0, CW]), ALU.mult).then_inc(y_out_ready, 1)

            last_two = [KT - 2, KT - 1]
            last_x(0, KT - 2)
            last_x(0, KT - 1)
            last_sum(0, last_two)
            dve.wait_ge(f_std_ready, 1)
            link(v.reciprocal(row_rstd[:, cols(0)], row_rstd[:, cols(0)]))
            last_x(1, KT - 2)
            norm(row_rstd[:, cols(0)])
            last_x(1, KT - 1)
            last_sum(1, last_two)
            norm(row_rstd[:, cols(0)])
            last_x(2, KT - 2)
            inverse(1)
            last_sum(2, [KT - 2])
            dve.wait_ge(f_spread, 1)
            norm(aux[:, 1, 0:CW])
            last_x(2, KT - 1)
            norm(aux[:, 1, 0:CW])
            inverse(2)
            dve.wait_ge(f_spread, 2)
            for _ in range(4):
                norm(aux[:, 0, 0:CW])


def kernel(**inputs):
    import numpy as np
    import concourse.bacc as bacc
    from concourse.bass_utils import run_bass_kernel_spmd

    a = {k: np.asarray(v) for k, v in inputs.items()}
    cat = np.concatenate

    def channel_major(x):
        return x.T.reshape(KT, P, -1).transpose(1, 0, 2)

    def column_blocks(w, width=P):
        k, n = w.shape
        return w.reshape(k // P, P, n // width, width).transpose(2, 1, 0, 3).reshape(n // width, P, -1)

    w_in = {kind: column_blocks(a["w_in"][0][:, part * D:(part + 1) * D]) for kind, part in W_IN_PART.items()}
    main = [w_in[kind][2 * g + tile] for g in range(PAIRS) for kind, tile, _ in PAIR_JOBS if kind != "pool_mix"]
    main = cat([np.stack(main), column_blocks(a["w_b_out"][0]), column_blocks(a["w_a_out"][0]), column_blocks(a["w_out"][0])])
    mix = cat([column_blocks(a["w_grp"][0][g]) for g in range(PAIRS)])

    w_ada, b_ada = a["w_ada"][0], a["b_ada"][0]
    order = [np.arange(part * D + 2 * q * P, part * D + (2 * q + 2) * P) for q in range(PAIRS) for part in (0, 1)]
    order = cat(order + [np.arange(2 * D, 3 * D)])
    ada = column_blocks(w_ada[:, order], ADA_CHUNK).reshape(6, P, KT, ADA_CHUNK)
    ada_b = b_ada[order].reshape(6, ADA_BLOCKS, P).transpose(2, 0, 1)

    def column(x):
        return x.reshape(KT, P).T

    par = cat([a["w_dw"][0], a["b_dw"], a["pool_scale"]])
    par = channel_major(par).reshape(P, PAIRS, 2, N_PAR)
    poolc = np.zeros((P, PAIRS, N_POOLC), np.float32)
    for g in range(PAIRS):
        w = 2 << g
        poolc[:, g, 0:g + 1] = 1.0
        poolc[:, g, DOUBLINGS] = 1.0 / w
        poolc[:, g, DOUBLINGS + 1:DOUBLINGS + 1 + POOL_MAX] = 1.0 / np.minimum(np.arange(POOL_MAX) + 1, w)
        poolc[:, g, N_POOLC - w:] = 1.0 / w

    def state(x):
        return x.transpose(2, 1, 0).reshape(KT, P, x.shape[1], NSAMP).transpose(1, 0, 2, 3)

    sent = {
        "x_t": channel_major(cat([a["x_prompt"][0], a["x_sample"][:, 0]])),
        "c_t": channel_major(cat([a["c_prompt"], a["c_sample"]])),
        "eye": np.eye(P, TOKB, dtype=np.float32),
        "pick": np.tile(np.eye(QUAD, NMOD, dtype=np.float32), (QUADS, 1)),
        "w_ada": ada, "ada_b": ada_b, "w_main": main, "w_mix": mix,
        "vecs": np.stack([column(a["g_norm"][0]), column(a["ln_g"][0]), column(a["ln_b"][0]), column(a["g_final"])], 1),
        "par": par, "poolc": poolc,
        "state_conv": state(a["state_conv"][0]), "state_pool": state(a["state_pool"][0]),
    }
    sent = {k: np.ascontiguousarray(v) for k, v in sent.items()}
    nc = bacc.Bacc("TRN2", target_bir_lowering=False, num_devices=1)
    t = {k: nc.dram_tensor(k, v.shape, F32, kind="ExternalInput").ap() for k, v in sent.items()}
    outs = {"y": [P, KT, TOK], "conv_p": [P, KT, CONV_BUF], "conv_s": [P, KT, CONV_BUF, NSAMP],
            "pool_p": [P, KT, POOL_BUF], "pool_s": [P, KT, POOL_BUF, NSAMP]}
    for k, shape in outs.items():
        t[k] = nc.dram_tensor(k, shape, F32, kind="ExternalOutput").ap()
    for k in ("y_conv", "sig_a", "sig_b", "silu_z"):
        t[k] = nc.dram_tensor(k, [P, KT, TOK], F32, kind="Internal").ap()
    build(nc, t)
    r = run_bass_kernel_spmd(nc, [sent], core_ids=[0]).results[0]

    def rows(x):
        return x.transpose(2, 1, 0).reshape(x.shape[2], D)

    y = rows(r["y"])
    samples = {k: r[k].transpose(3, 2, 1, 0).reshape(1, NSAMP, -1, D) for k in ("conv_s", "pool_s")}
    return (y[None, :SEQ], y[SEQ:, None], rows(r["conv_p"])[None, None], samples["conv_s"],
            rows(r["pool_p"])[None, None], samples["pool_s"])
```
